# Optimizing a Trainium2 kernel written in Bass

```python
import math
import jax, jax.numpy as jnp
from jax import lax
import numpy as np

D_MODEL = 1024
BATCH = 1
SEQ = 256
DEPTH = 1
DEC_BATCH = 8
DEC_SEQ = 8
PAST_LEN = 2048
PAGE_SIZE = 128

D_MIX = D_MODEL
CONV_W = D_MIX // 2
CONV_GROUPS = 8
CONV_K = 3
LRU_W = D_MIX - CONV_W
LRU_HEADS = 8
LRU_HEAD_DIM = LRU_W // LRU_HEADS
LRU_CONV_K = 4
LRU_C = 8.0
N_EXPERTS = 32
TOP_K = 4
D_FF = D_MODEL
SWIGLU_LIMIT = 7.0
SWIGLU_ALPHA = 1.702
MOE_BLOCK = 128
LN_EPS = 1e-5
RMS_EPS = 1e-6
DEEPNORM_ALPHA = (2.0 * DEPTH) ** 0.25
DEEPNORM_BETA = (8.0 * DEPTH) ** -0.25
IN_COLS = 3 * CONV_W + 2 * LRU_W

kernel_name = "hybrid_conv_rglru_moe_decoder_step"

def _layer_norm(x, g, b):
    xf = x.astype(jnp.float32)
    mu = jnp.mean(xf, axis=-1, keepdims=True)
    var = jnp.mean(jnp.square(xf - mu), axis=-1, keepdims=True)
    y = (xf - mu) * lax.rsqrt(var + LN_EPS) * g.astype(jnp.float32) + b.astype(jnp.float32)
    return y.astype(x.dtype)

def _rms_norm(x, g):
    xf = x.astype(jnp.float32)
    y = xf * lax.rsqrt(jnp.mean(jnp.square(xf), axis=-1, keepdims=True) + RMS_EPS) * g.astype(jnp.float32)
    return y.astype(x.dtype)

def _causal_dwconv(u, buf, w):
    k = w.shape[0]
    s = u.shape[1]
    full = jnp.concatenate([buf.astype(u.dtype), u], axis=1)
    y = full[:, 0:s] * w[0]
    for j in range(1, k):
        y = y + full[:, j:j + s] * w[j]
    return y, full[:, -(k - 1):]

def _lin_comb(left, right):
    a1, b1 = left
    a2, b2 = right
    return a1 * a2, a2 * b1 + b2

def _rg_lru(xr, h0, wa, ba, wi, bi, lam):
    bsz, s, _ = xr.shape
    xh = xr.reshape(bsz, s, LRU_HEADS, LRU_HEAD_DIM)
    r = jax.nn.sigmoid(jnp.einsum('bshi,hij->bshj', xh, wa).reshape(bsz, s, LRU_W) + ba)
    i = jax.nn.sigmoid(jnp.einsum('bshi,hij->bshj', xh, wi).reshape(bsz, s, LRU_W) + bi)
    log_a = (-LRU_C * r.astype(jnp.float32)) * jax.nn.softplus(-lam.astype(jnp.float32))
    a = jnp.exp(log_a)
    mult = jnp.sqrt(-jnp.expm1(2.0 * log_a))
    bvals = (xr * i).astype(jnp.float32) * mult
    a_cum, b_cum = lax.associative_scan(_lin_comb, (a, bvals), axis=1)
    h = a_cum * h0.astype(jnp.float32)[:, None, :] + b_cum
    return h.astype(xr.dtype), h[:, -1].astype(xr.dtype)

def _mixer(x, buf_a, buf_b, h0, w_in, conv_a_w, conv_b_w, conv_b_b,
           lru_wa, lru_ba, lru_wi, lru_bi, lru_lambda, gn_a, gn_b, w_out):
    u = x @ w_in
    xa, gate_b, gate_c, xl, gl = jnp.split(u, [CONV_W, 2 * CONV_W, 3 * CONV_W, 3 * CONV_W + LRU_W], axis=-1)
    ya, new_a = _causal_dwconv(gate_c * xa, buf_a, conv_a_w)
    ya = gate_b * ya
    xc, new_b = _causal_dwconv(xl, buf_b, conv_b_w)
    xc = xc + conv_b_b
    h, h_last = _rg_lru(xc, h0, lru_wa, lru_ba, lru_wi, lru_bi, lru_lambda)
    yb = h * jax.nn.gelu(gl)
    mix = jnp.concatenate([_rms_norm(ya, gn_a), _rms_norm(yb, gn_b)], axis=-1) @ w_out
    return mix, new_a, new_b, h_last

def _moe(x, router_w, router_b, wg, bg, wu, bu, wd, bd):
    shp = x.shape
    xt = x.reshape(-1, D_MODEL)
    t = xt.shape[0]
    logits = (xt @ router_w + router_b).astype(jnp.float32)
    top_v, top_i = lax.top_k(logits, TOP_K)
    gate = jax.nn.softmax(top_v, axis=-1)
    n_assign = t * TOP_K
    flat_e = top_i.reshape(-1)
    flat_tok = jnp.repeat(jnp.arange(t, dtype=jnp.int32), TOP_K)
    flat_w = gate.reshape(-1)
    order = jnp.argsort(flat_e)
    sorted_e = flat_e[order]
    counts = jnp.bincount(flat_e, length=N_EXPERTS)
    padded = (counts + MOE_BLOCK - 1) // MOE_BLOCK * MOE_BLOCK
    start = jnp.cumsum(counts) - counts
    pend = jnp.cumsum(padded)
    pstart = pend - padded
    rank = jnp.arange(n_assign, dtype=jnp.int32) - start[sorted_e]
    dest = pstart[sorted_e] + rank
    n_blocks = -(-n_assign // MOE_BLOCK) + N_EXPERTS
    p = n_blocks * MOE_BLOCK
    tok_buf = jnp.full((p,), t, dtype=jnp.int32).at[dest].set(flat_tok[order])
    w_buf = jnp.zeros((p,), jnp.float32).at[dest].set(flat_w[order])
    block_start = jnp.arange(n_blocks, dtype=jnp.int32) * MOE_BLOCK
    block_expert = jnp.minimum(jnp.searchsorted(pend, block_start, side='right'), N_EXPERTS - 1)
    x_pad = jnp.concatenate([xt, jnp.zeros((1, D_MODEL), xt.dtype)], axis=0)
    xb = x_pad[tok_buf].reshape(n_blocks, MOE_BLOCK, D_MODEL)

    def expert_block(args):
        xblk, e = args
        g = xblk @ wg[e] + bg[e]
        up = xblk @ wu[e] + bu[e]
        g = jnp.minimum(g, SWIGLU_LIMIT)
        up = jnp.clip(up, -SWIGLU_LIMIT, SWIGLU_LIMIT)
        glu = g * jax.nn.sigmoid(SWIGLU_ALPHA * g)
        return ((up + 1.0) * glu) @ wd[e] + bd[e]

    yb = lax.map(expert_block, (xb, block_expert))
    out = jnp.zeros((t + 1, D_MODEL), jnp.float32).at[tok_buf].add(
        yb.reshape(p, D_MODEL).astype(jnp.float32) * w_buf[:, None])
    return out[:t].astype(x.dtype).reshape(shp)

def _layer(x, buf_a, buf_b, h0, w_in, conv_a_w, conv_b_w, conv_b_b, lru_wa, lru_ba, lru_wi, lru_bi,
           lru_lambda, gn_a, gn_b, w_out, ln1_g, ln1_b, router_w, router_b,
           exp_w_gate, exp_b_gate, exp_w_up, exp_b_up, exp_w_down, exp_b_down, ln2_g, ln2_b):
    mix, new_a, new_b, h_last = _mixer(x, buf_a, buf_b, h0, w_in, conv_a_w, conv_b_w, conv_b_b,
                                       lru_wa, lru_ba, lru_wi, lru_bi, lru_lambda, gn_a, gn_b, w_out)
    x = _layer_norm(DEEPNORM_ALPHA * x + mix, ln1_g, ln1_b)
    ff = _moe(x, router_w, router_b, exp_w_gate, exp_b_gate, exp_w_up, exp_b_up, exp_w_down, exp_b_down)
    x = _layer_norm(DEEPNORM_ALPHA * x + ff, ln2_g, ln2_b)
    return x, new_a, new_b, h_last

def setup_inputs(seed: int = 0) -> dict:
    key = jax.random.key(seed)
    ks = jax.random.split(key, 32)
    f32 = jnp.float32
    nrm = lambda k, shp, sc: jax.random.normal(k, shp, f32) * sc
    a0 = jax.random.uniform(ks[12], (DEPTH, LRU_W), f32, 0.9, 0.999)
    return {
        "x_prompt": nrm(ks[0], (BATCH, SEQ, D_MODEL), 1.0),
        "x_sample": nrm(ks[1], (DEC_BATCH, DEC_SEQ, D_MODEL), 1.0),
        "state_conv_a": nrm(ks[2], (DEPTH, DEC_BATCH, CONV_K - 1, CONV_W), 1.0),
        "state_conv_b": nrm(ks[3], (DEPTH, DEC_BATCH, LRU_CONV_K - 1, LRU_W), 1.0),
        "state_lru_h": nrm(ks[4], (DEPTH, DEC_BATCH, LRU_W), 0.5),
        "w_in": nrm(ks[5], (DEPTH, D_MODEL, IN_COLS), D_MODEL ** -0.5),
        "conv_a_w": nrm(ks[6], (DEPTH, CONV_K, CONV_W), CONV_K ** -0.5),
        "conv_b_w": nrm(ks[7], (DEPTH, LRU_CONV_K, LRU_W), LRU_CONV_K ** -0.5),
        "conv_b_b": nrm(ks[8], (DEPTH, LRU_W), 0.02),
        "lru_wa": nrm(ks[9], (DEPTH, LRU_HEADS, LRU_HEAD_DIM, LRU_HEAD_DIM), LRU_HEAD_DIM ** -0.5),
        "lru_ba": nrm(ks[10], (DEPTH, LRU_W), 0.1),
        "lru_wi": nrm(ks[11], (DEPTH, LRU_HEADS, LRU_HEAD_DIM, LRU_HEAD_DIM), LRU_HEAD_DIM ** -0.5),
        "lru_bi": nrm(ks[13], (DEPTH, LRU_W), 0.1),
        "lru_lambda": jnp.log(a0) - jnp.log1p(-a0),
        "gn_a": 1.0 + nrm(ks[14], (DEPTH, CONV_W), 0.02),
        "gn_b": 1.0 + nrm(ks[15], (DEPTH, LRU_W), 0.02),
        "w_out": nrm(ks[16], (DEPTH, D_MIX, D_MODEL), DEEPNORM_BETA * D_MIX ** -0.5),
        "ln1_g": 1.0 + nrm(ks[17], (DEPTH, D_MODEL), 0.02),
        "ln1_b": nrm(ks[18], (DEPTH, D_MODEL), 0.02),
        "router_w": nrm(ks[19], (DEPTH, D_MODEL, N_EXPERTS), D_MODEL ** -0.5),
        "router_b": nrm(ks[20], (DEPTH, N_EXPERTS), 0.01),
        "exp_w_gate": nrm(ks[21], (DEPTH, N_EXPERTS, D_MODEL, D_FF), D_MODEL ** -0.5),
        "exp_b_gate": nrm(ks[22], (DEPTH, N_EXPERTS, D_FF), 0.02),
        "exp_w_up": nrm(ks[23], (DEPTH, N_EXPERTS, D_MODEL, D_FF), D_MODEL ** -0.5),
        "exp_b_up": nrm(ks[24], (DEPTH, N_EXPERTS, D_FF), 0.02),
        "exp_w_down": nrm(ks[25], (DEPTH, N_EXPERTS, D_FF, D_MODEL), DEEPNORM_BETA * D_FF ** -0.5),
        "exp_b_down": nrm(ks[26], (DEPTH, N_EXPERTS, D_MODEL), 0.02),
        "ln2_g": 1.0 + nrm(ks[27], (DEPTH, D_MODEL), 0.02),
        "ln2_b": nrm(ks[28], (DEPTH, D_MODEL), 0.02),
    }

def reference(x_prompt, x_sample, state_conv_a, state_conv_b, state_lru_h,
              w_in, conv_a_w, conv_b_w, conv_b_b, lru_wa, lru_ba, lru_wi, lru_bi, lru_lambda,
              gn_a, gn_b, w_out, ln1_g, ln1_b, router_w, router_b,
              exp_w_gate, exp_b_gate, exp_w_up, exp_b_up, exp_w_down, exp_b_down, ln2_g, ln2_b):
    xp = x_prompt
    xs = x_sample
    pa, pb, ph, sa, sb, sh = [], [], [], [], [], []
    for l in range(DEPTH):
        w = (w_in[l], conv_a_w[l], conv_b_w[l], conv_b_b[l], lru_wa[l], lru_ba[l], lru_wi[l], lru_bi[l],
             lru_lambda[l], gn_a[l], gn_b[l], w_out[l], ln1_g[l], ln1_b[l], router_w[l], router_b[l],
             exp_w_gate[l], exp_b_gate[l], exp_w_up[l], exp_b_up[l], exp_w_down[l], exp_b_down[l],
             ln2_g[l], ln2_b[l])
        zb_a = jnp.zeros((xp.shape[0], CONV_K - 1, CONV_W), xp.dtype)
        zb_b = jnp.zeros((xp.shape[0], LRU_CONV_K - 1, LRU_W), xp.dtype)
        zh = jnp.zeros((xp.shape[0], LRU_W), xp.dtype)
        xp, na, nb, nh = _layer(xp, zb_a, zb_b, zh, *w)
        pa.append(na); pb.append(nb); ph.append(nh)
        xs, na, nb, nh = _layer(xs, state_conv_a[l], state_conv_b[l], state_lru_h[l], *w)
        sa.append(na); sb.append(nb); sh.append(nh)
    prompt_conv_a = jnp.stack(pa)
    prompt_conv_b = jnp.stack(pb)
    prompt_lru_h = jnp.stack(ph)
    sample_conv_a = jnp.stack(sa)
    sample_conv_b = jnp.stack(sb)
    sample_lru_h = jnp.stack(sh)
    return (xp, xs, prompt_conv_a, prompt_conv_b, prompt_lru_h, sample_conv_a, sample_conv_b, sample_lru_h)


_drawn_inputs = setup_inputs


def setup_inputs(seed=0):
    import zlib

    import numpy as np

    out = dict(_drawn_inputs(seed))
    spreads = {}
    factors = {'gn_a': 3.496,
     'gn_b': 3.107,
     'exp_b_gate': 8.0,
     'exp_b_up': 8.0,
     'exp_b_down': 6.406,
     'ln2_g': 9.642,
     'ln2_b': 8.505,
     'router_b': 3.718}
    for name, (base, spread) in spreads.items():
        noise = np.random.default_rng([zlib.crc32(name.encode()), seed]).standard_normal(out[name].shape)
        drawn = base * np.exp(spread * noise) if base else spread * noise
        out[name] = __import__('jax').numpy.asarray(drawn.astype(out[name].dtype))
    for name, factor in factors.items():
        out[name] = (out[name] * factor).astype(out[name].dtype)
    return out
```

```python
import math
from contextlib import ExitStack

import concourse.bass as bass
from concourse import mybir

P = 128
D = 1024
CH = D // P
SEQ = 256
NB, DS = 8, 8
T = SEQ + NB * DS
TILES = [(0, 128), (128, 128), (256, 64)]
CW = 512
CT = CW // P
HIST = 3
SEG = HIST + DS
S0 = HIST + SEQ
FW = S0 + NB * SEG
OW = FW - HIST
NE, TOPK = 32, 4
UT = 64
MAXU = NE + T * TOPK // UT
TABW = MAXU + 1
HALF = D // 2
SLOTW = 4 * D
NSLOT = 6
EMPTY = 65536.0
ALPHA = 2.0 ** 0.25
LIMIT, SWISH = 7.0, 1.702
LN_EPS, RMS_EPS = 1e-5, 1e-6
LRU_C = 8.0
GELU_A, GELU_B = 0.044715, math.sqrt(2.0 / math.pi)

ROW_WA, ROW_WB, ROW_CB, ROW_BA, ROW_BI, ROW_LAM, ROW_GA, ROW_GB = 0, 3, 7, 8, 9, 10, 11, 12
ROW_SA, ROW_SB, ROW_H0, ROWS = 13, 29, 53, 61
OUT_PA, OUT_PB, OUT_PH, OUT_SA, OUT_SB, OUT_SH, OUTS = 0, 2, 5, 6, 22, 46, 54

IN_GROUPS = [(3, 3), (4, 4), (2, 5), (0, 3), (1, 4)]
PRIOR = [0, 0, 0, 3, 2, 2]


def hybrid_layer(nc, a):
    fp32, bf16, i32, u32 = mybir.dt.float32, mybir.dt.bfloat16, mybir.dt.int32, mybir.dt.uint32
    ALU, ACT, AX = mybir.AluOpType, mybir.ActivationFunctionType, mybir.AxisListType
    with ExitStack() as ctx:
        def sb(name, shape, dt=fp32):
            return ctx.enter_context(nc.sbuf_tensor(name, shape, dt))

        def sem(name):
            return ctx.enter_context(nc.semaphore(name))

        ring = sb("ring", [P, NSLOT, SLOTW])
        x = sb("x", [P, 3, D])
        xT = sb("xT", [P, CH, T])
        ident = sb("ident", [P, P])
        ones = sb("ones", [P, P])
        ones_bf = sb("ones_bf", [P, P], bf16)
        earlier_bf = sb("earlier_bf", [P, P], bf16)
        half_sel = sb("half_sel", [2, P])
        half_col = sb("half_col", [P, 1])
        iota_i = sb("iota_i", [P, P], i32)
        iota_e = sb("iota_e", [P, NE])
        iota_u = sb("iota_u", [P, TABW])
        iota_s = sb("iota_s", [P, P])
        tok_val = sb("tok_val", [P, 3])
        router_w = sb("router_w", [P, CH, NE])
        router_b = sb("router_b", [P, NE])
        ln_g = sb("ln_g", [P, D])
        ln_b = sb("ln_b", [P, D])
        stats = sb("stats", [P, 3, 12])
        mean_var = sb("mean_var", [P, 3, 2])
        rstd = sb("rstd", [P, 3])
        shift = sb("shift", [P, 3])
        unit_rows = sb("unit_rows", [P, TABW], i32)
        unit_gate = sb("unit_gate", [P, TABW])
        unit_info = sb("unit_info", [1, TABW + 1], i32)
        rows_g = sb("rows_g", [P, 1], i32)
        rows_s = sb("rows_s", [P, 1], i32)

        AREA = 15600
        area = sb("area", [P, AREA])
        at = [0]

        def carve(parts, *dims, dt=fp32):
            n = math.prod(dims)
            v = area[0:parts, at[0]:at[0] + n]
            at[0] += n
            assert at[0] <= AREA, at[0]
            if dt != fp32:
                v = v.bitcast(dt)
            if len(dims) == 2:
                v = v.rearrange("p (a b) -> p a b", b=dims[1])
            elif len(dims) == 3:
                v = v.rearrange("p (a b c) -> p a b c", b=dims[1], c=dims[2])
            return v

        xl_pad = carve(P, CT, FW)
        cv_pad = carve(P, CT, FW)
        xc = carve(P, CT, OW)
        decay = carve(P, CT, OW)
        drive = carve(P, CT, OW)
        mult = carve(P, CT, OW)
        gate_c = carve(P, CT, T)
        gl = carve(P, CT, T)
        tmp = carve(P, CT, OW)
        conv_a = mult
        params = carve(ROWS, CW)
        chan = carve(P, CT, 64)
        lam8 = carve(P, 2, CT)
        small = carve(P, 8, CT)
        wa_bd = carve(P, CT, P)
        wi_bd = carve(P, CT, P)
        rms = carve(P, T)
        states = carve(P, CT, 64)
        states_out = carve(OUTS, CW)
        mixer_end = at[0]
        mixT = sb("mixT", [P, CH, T])
        at[0] = 0
        scaled = carve(P, 3, D)
        logits = carve(P, 3, NE)
        top_v = carve(P, 3, 8)
        top_i = carve(P, 3, 8)
        top_f = carve(P, 3, TOPK)
        gates = carve(P, 3, TOPK)
        gsum = carve(P, 6)
        onehot = carve(P, 3, TOPK * NE)
        chosen_f = carve(P, 3, NE)
        counts = carve(P, NE)
        n_units = carve(P, NE)
        ends = carve(P, NE)
        zeros_e = carve(P, NE)
        first = carve(P, NE)
        pos = carve(P, 3, NE)
        picked = carve(P, 3, TOPK * NE)
        place = carve(P, 3, TOPK)
        slot_f = carve(P, 3, TOPK)
        unit_f = carve(P, 3, TOPK)
        slot_hot = carve(P, 3 * TOPK, P)
        unit_val = carve(P, 3 * TOPK, 2 * TABW)
        row_f = carve(P, 2, TABW)
        before = carve(1, TABW, NE)
        x_rows = carve(P, HALF)
        xTu = carve(P, HALF)
        hTu = carve(P, HALF)
        g_min = carve(P, HALF)
        up_clip = carve(P, HALF)
        sig = carve(P, HALF)
        hid = carve(P, HALF)
        y_rows = carve(P, HALF)
        bias_rows = carve(2, 3, HALF)
        place_i = sb("place_i", [P, 3, TOPK], i32)
        slot_i = sb("slot_i", [P, 3, TOPK], i32)
        unit_i = sb("unit_i", [P, 3, TOPK], i32)
        chosen = sb("chosen", [P, 3, NE], bf16)
        final = ring[:, 0, 0:3 * D].rearrange("p (t n) -> p t n", n=D)

        bank = [ctx.enter_context(nc.psum_tensor(f"bank{i}", [P, 512], fp32)) for i in range(8)]
        x1_rows = nc.dram_tensor("x1_rows", [2 * T, HALF], fp32).ap()
        acc_rows = nc.dram_tensor("acc_rows", [2 * T, HALF], fp32).ap()

        def tokens(dram, t):
            first_tok, n = TILES[t]
            return dram[2 * first_tok:2 * (first_tok + n), :].rearrange("(t h) n -> t (h n)", h=2)

        S = {n: sem(n) for n in (
            "x_in params_in gatew_in router_in ln1_in ln2_in acc_in acc_written "
            "ident_ok consts_ok pads_ok bd_zero hist_ok "
            "xt_psum xt_dve xt_act chan_psum chan_ok lam_abs lam_exp lam_w lam_ln lam_ok "
            "proj_done xl_ok gl_ok c_ok bank_dve xc_ok gates_psum sig_ok gelu_in gelu_t ath_ok one_m mult_ok "
            "h_ok sqb_ok rmsb_psum rmsb_in rmsb_ok yb_ok sqa_ok rmsa_psum rmsa_in rmsa_ok ya_ok "
            "cv_ok states_ok states_psum states_sb states_dma "
            "lru_rows_used out_psum var_ok rstd_ok shift_ok norm_ok x1_ok scaled_ok x1_dma "
            "x1t_psum x1t_dve x1t_act logit_psum top_ok exp_ok chosen_ok rank_psum pos_ok hot_ok tab_psum tab_ok "
            "first_idx gath_idx gathered scat_idx bias_in bias_used "
            "gate_done gate_free up_done up_free sig_done glu_ok hid_ok "
            "xu_psum xu_ok hu_psum hu_ok y_done y_ok "
            "ln2_var ln2_rstd ln2_norm ln2_ok out_dma dve_step act_step pool_step").split()}
        slot_loaded = [sem(f"slot_loaded{i}") for i in range(NSLOT)]
        half_used = [sem(f"half_used{m}") for m in range(3)]
        product_done = ["gate_done", "up_done", "y_done"]

        block = ctx.enter_context(nc.Block())
        w_in_v = a["w_in"][0].rearrange("(c p) n -> p c n", p=P)
        w_out_v = a["w_out"][0].rearrange("(c p) n -> p c n", p=P)
        experts = [a["exp_w_gate"][0], a["exp_w_up"][0], a["exp_w_down"][0]]
        biases = [a["exp_b_gate"][0], a["exp_b_up"][0], a["exp_b_down"][0]]

        def slot_src(s, e):
            m = experts[s // 2]
            rows = m[e, (s % 2) * HALF:(s % 2 + 1) * HALF, :] if isinstance(e, int) else \
                m[bass.ds(e, 1), (s % 2) * HALF:(s % 2 + 1) * HALF, :].rearrange("o k n -> (o k) n")
            return rows.rearrange("(c p) n -> p c n", p=P)

        def slot(s):
            return ring[:, s, :].rearrange("p (c n) -> p c n", n=D)

        def sample_cols(v_, j):
            w_ = v_[:, j, S0:OW]
            return bass.AP(tensor=w_.tensor, offset=w_.offset, ap=[w_.ap[0], (SEG, NB), (1, DS)])

        def x1_side(act, s_, t):
            n = TILES[t][1]
            act.wait_ge(S["x1_ok"], t + 1)
            s_.mul(scaled[0:n, t, :], x[0:n, t, :], ALPHA).then_inc(S["scaled_ok"], 1)
            if t < 2:
                act.wait_ge(S["x1t_psum"], t + 1)
                s_.copy(xT[:, 4:8, t * P:(t + 1) * P],
                        bank[(7, 3)[t]][:, :].rearrange("p (c n) -> p c n", c=4)).then_inc(S["x1t_act"], 1)

        @block.sync
        def _(sp):
            for t, (t0, n) in enumerate(TILES):
                src = a["x_prompt"][0, t0:t0 + n, :] if t < 2 else a["x_sample"].rearrange("b s d -> (b s) d")
                sp.dma_start(x[0:n, t, :], src).then_inc(S["x_in"], 16)
            for g, s in IN_GROUPS[:3]:
                sp.dma_start(ring[:, s, :].rearrange("p (c n) -> p c n", n=CW),
                             w_in_v[:, :, g * CW:(g + 1) * CW]).then_inc(slot_loaded[s], 16)
            for s in range(3):
                sp.dma_start(slot(s), slot_src(s, 0)).then_inc(slot_loaded[s], 16)
            for i, (g, s) in enumerate(IN_GROUPS[3:]):
                sp.wait_ge(S["proj_done"], CT * (i + 1))
                sp.dma_start(ring[:, s, :].rearrange("p (c n) -> p c n", n=CW),
                             w_in_v[:, :, g * CW:(g + 1) * CW]).then_inc(slot_loaded[s], 16)
            sp.wait_ge(S["proj_done"], 3 * CT)
            sp.dma_start(slot(5), w_out_v[:, CT:CH, :]).then_inc(slot_loaded[5], 16)
            sp.wait_ge(S["proj_done"], 4 * CT)
            sp.dma_start(slot(3), w_out_v[:, 0:CT, :]).then_inc(slot_loaded[3], 16)
            for s, done, count in ((4, "proj_done", 5 * CT), (5, "lru_rows_used", 1), (3, "out_psum", 3)):
                sp.wait_ge(S[done], count)
                sp.dma_start(slot(s), slot_src(s, 0)).then_inc(slot_loaded[s], 16)
            for t, (t0, n) in enumerate(TILES):
                sp.wait_ge(S["x1_ok"], t + 1)
                sp.dma_start(tokens(x1_rows, t), x[0:n, t, :]).then_inc(S["x1_dma"], 16)
            for v, name in ((ln_g, "ln2_g"), (ln_b, "ln2_b")):
                sp.dma_start(v[:, :], a[name].partition_broadcast(P).rearrange("p o n -> p (o n)"))\
                    .then_inc(S["ln2_in"], 16)
            sp.wait_ge(S["tab_ok"], 1)
            n_unit = sp.value_load(unit_info[0:1, TABW:TABW + 1], min_val=NE, max_val=MAXU)
            with sp.Fori(1, n_unit) as u:
                e = sp.value_load(unit_info[0:1, bass.ds(u, 1)], min_val=0, max_val=NE - 1)
                for s in range(NSLOT):
                    sp.wait_ge(half_used[s // 2] if s % 2 == 0 else S[product_done[s // 2]], u)
                    sp.dma_start(slot(s), slot_src(s, e)).then_inc(slot_loaded[s], 16)
            sp.wait_ge(S["acc_written"], n_unit * 16 + 48)
            for t, (t0, n) in enumerate(TILES):
                sp.dma_start(final[0:n, t, :], tokens(acc_rows, t)).then_inc(S["acc_in"], 16)
            for t, (t0, n) in enumerate(TILES):
                sp.wait_ge(S["ln2_ok"], t + 1)
                dst = a["y_prompt"][0, t0:t0 + n, :] if t < 2 else a["y_sample"].rearrange("b s d -> (b s) d")
                sp.dma_start(dst, final[0:n, t, :]).then_inc(S["out_dma"], 16)
            sp.wait_ge(S["out_dma"], 48)
            sp.wait_ge(S["states_dma"], 96)

        @block.gpsimd
        def _(pool):
            g = nc.gpsimd
            step = [0]

            def settle(ins):
                step[0] += 1
                ins.then_inc(S["pool_step"], 1)
                pool.wait_ge(S["pool_step"], step[0])

            settle(g.memset(ident[:, :], 0.0))
            g.affine_select(out=ident[:, :], in_=ident[:, :], compare_op=ALU.not_equal, fill=1.0, base=0,
                            pattern=[[-1, P]], channel_multiplier=1).then_inc(S["ident_ok"], 1)
            g.memset(wa_bd, 0.0).then_inc(S["bd_zero"], 1)
            g.memset(wi_bd, 0.0).then_inc(S["bd_zero"], 1)
            g.memset(xl_pad, 0.0).then_inc(S["pads_ok"], 1)
            g.memset(cv_pad, 0.0).then_inc(S["pads_ok"], 1)
            pool.wait_ge(S["pads_ok"], 2)
            pool.wait_ge(S["chan_ok"], 1)
            samples = slice(S0, FW)

            for j in range(CT):
                last = g.tensor_copy(
                    xl_pad[:, j, samples].rearrange("p (b s) -> p b s", s=SEG)[:, :, 0:3],
                    chan[:, j, ROW_SB:ROW_SB + 3 * NB].rearrange("p (b k) -> p b k", k=3))
                last = g.tensor_copy(
                    cv_pad[:, j, samples].rearrange("p (b s) -> p b s", s=SEG)[:, :, 1:3],
                    chan[:, j, ROW_SA:ROW_SA + 2 * NB].rearrange("p (b k) -> p b k", k=2))
                last.then_inc(S["hist_ok"], 1)
            g.memset(ones[:, :], 1.0).then_inc(S["consts_ok"], 1)
            settle(g.memset(ones_bf[:, :], 1.0))
            g.affine_select(out=earlier_bf[:, :], in_=ones_bf[:, :], compare_op=ALU.is_gt, fill=0.0, base=0,
                            pattern=[[1, P]], channel_multiplier=-1).then_inc(S["consts_ok"], 1)
            pool.wait_ge(S["consts_ok"], 2)
            g.affine_select(out=half_col[:, :], in_=ones[:, 0:1], compare_op=ALU.is_ge, fill=0.0, base=-UT,
                            pattern=[[0, 1]], channel_multiplier=1).then_inc(S["consts_ok"], 1)
            settle(g.affine_select(out=half_sel[:, :], in_=ones[0:2, :], compare_op=ALU.is_ge, fill=0.0,
                                   base=0, pattern=[[1, P]], channel_multiplier=-UT))
            g.affine_select(out=half_sel[:, :], in_=half_sel[:, :], compare_op=ALU.is_ge, fill=0.0,
                            base=UT - 1, pattern=[[-1, P]], channel_multiplier=UT).then_inc(S["consts_ok"], 1)
            settle(g.iota(iota_i[:, :], pattern=[[1, P]], base=0, channel_multiplier=0))
            g.tensor_copy(iota_e[:, :], iota_i[:, 0:NE]).then_inc(S["consts_ok"], 1)
            g.tensor_copy(iota_s[:, 0:UT], iota_i[:, 0:UT]).then_inc(S["consts_ok"], 1)
            g.tensor_copy(iota_s[:, UT:P], iota_i[:, 0:UT]).then_inc(S["consts_ok"], 1)
            settle(g.tensor_copy(iota_u[:, :], iota_i[:, 0:TABW]))
            settle(g.iota(iota_i[:, 0:3], pattern=[[P, 3]], base=1, channel_multiplier=1))
            g.tensor_copy(tok_val[:, :], iota_i[:, 0:3]).then_inc(S["consts_ok"], 1)

            def put(col, n, src):
                return g.tensor_copy(states[:, :, col:col + n], src)

            def put_samples(j, col, n, src, first_col):
                return g.tensor_copy(
                    states[:, j, col:col + n * NB].rearrange("p (b k) -> p b k", k=n),
                    src.rearrange("p (b s) -> p b s", s=SEG)[:, :, first_col:first_col + n])

            pool.wait_ge(S["xl_ok"], CT)
            put(OUT_PB, 3, xl_pad[:, :, S0 - 3:S0])
            for j in range(CT):
                put_samples(j, OUT_SB, 3, xl_pad[:, j, samples], SEG - 3)
            pool.wait_ge(S["h_ok"], 1)
            put(OUT_PH, 1, xc[:, :, SEQ - 1:SEQ])
            for j in range(CT):
                g.tensor_copy(states[:, j, OUT_SH:OUT_SH + NB], xc[:, j, S0 + DS - 1:OW:SEG])
            pool.wait_ge(S["cv_ok"], 4 * 2)
            put(OUT_PA, 2, cv_pad[:, :, S0 - 2:S0])
            for j in range(CT):
                last = put_samples(j, OUT_SA, 2, cv_pad[:, j, samples], SEG - 2)
            last.then_inc(S["states_ok"], 1)

            for t, (t0, n) in enumerate(TILES):
                pool.wait_ge(S["scaled_ok"], t + 1)
                pool.dma_start(tokens(acc_rows, t), scaled[0:n, t, :]).then_inc(S["acc_written"], 16)

            pool.wait_ge(S["tab_ok"], 1)
            n_unit = pool.value_load(unit_info[0:1, TABW:TABW + 1], min_val=NE, max_val=MAXU)
            bound = pool.to_reg(2 * T - 1)
            g.memset(x_rows, 0.0).then_inc(S["first_idx"], 1)

            def gather(u):
                g.indirect_dma_start(out=x_rows, out_offset=None, in_=x1_rows[:, :],
                                     in_offset=bass.IndirectOffsetOnAxis(ap=rows_g[:, 0:1].bitcast(u32), axis=0),
                                     bounds_check=bound, oob_is_err=False).then_inc(S["gathered"], 16)

            def bias_load(e):
                for m in range(3):
                    src = biases[m][e, :].rearrange("(h n) -> h n", h=2) if isinstance(e, int) else \
                        biases[m][bass.ds(e, 1), :].rearrange("o (h n) -> (o h) n", h=2)
                    pool.dma_start(bias_rows[:, m, :], src).then_inc(S["bias_in"], 16)

            g.tensor_copy(rows_g[:, :], unit_rows[:, 0:1]).then_inc(S["first_idx"], 1)
            pool.wait_ge(S["x1_dma"], 48)
            pool.wait_ge(S["first_idx"], 2)
            gather(0)
            pool.wait_ge(S["states_dma"], 96)
            bias_load(0)
            with pool.Fori(0, n_unit) as u:
                u2 = pool.to_reg(u + 2)
                pool.wait_ge(S["gathered"], u * 16 + 16)
                g.tensor_copy(rows_g[:, :], unit_rows[:, bass.ds(u + 1, 1)]).then_inc(S["gath_idx"], 1)
                pool.wait_ge(S["x1_dma"], 48)
                pool.wait_ge(S["gath_idx"], u + 1)
                pool.wait_ge(S["xu_psum"], u + 1)
                gather(u + 1)
                e = pool.value_load(unit_info[0:1, bass.ds(u + 1, 1)], min_val=0, max_val=NE - 1)
                pool.wait_ge(S["bias_used"], u + 1)
                bias_load(e)
                pool.wait_ge(S["acc_written"], u * 16 + 48)
                g.tensor_copy(rows_s[:, :], unit_rows[:, bass.ds(u, 1)]).then_inc(S["scat_idx"], 1)
                pool.wait_ge(S["x1_dma"], 48)
                pool.wait_ge(S["scat_idx"], u + 1)
                pool.wait_ge(S["y_ok"], u2)
                g.indirect_dma_start(out=acc_rows[:, :],
                                     out_offset=bass.IndirectOffsetOnAxis(ap=rows_s[:, 0:1].bitcast(u32), axis=0),
                                     in_=y_rows, in_offset=None, bounds_check=bound, oob_is_err=False,
                                     compute_op=ALU.add).then_inc(S["acc_written"], 16)
            pool.wait_ge(S["gathered"], n_unit * 16 + 16)
            pool.wait_ge(S["bias_in"], n_unit * 48 + 48)
            pool.wait_ge(S["acc_written"], n_unit * 16 + 48)

        @block.scalar
        def _(act):
            s_ = nc.scalar
            step = [0]

            def settle(ins):
                step[0] += 1
                ins.then_inc(S["act_step"], 1)
                act.wait_ge(S["act_step"], step[0])

            for row, name, n in ((ROW_WA, "conv_a_w", 3), (ROW_WB, "conv_b_w", 4)):
                act.dma_start(params[row:row + n, :], a[name][0]).then_inc(S["params_in"], 16)
            for row, name in ((ROW_CB, "conv_b_b"), (ROW_BA, "lru_ba"), (ROW_BI, "lru_bi"), (ROW_LAM, "lru_lambda"),
                              (ROW_GA, "gn_a"), (ROW_GB, "gn_b")):
                act.dma_start(params[row:row + 1, :], a[name]).then_inc(S["params_in"], 16)
            act.dma_start(params[ROW_SA:ROW_SB, :], a["state_conv_a"][0].rearrange("b k c -> (b k) c"))\
                .then_inc(S["params_in"], 16)
            act.dma_start(params[ROW_SB:ROW_H0, :], a["state_conv_b"][0].rearrange("b k c -> (b k) c"))\
                .then_inc(S["params_in"], 16)
            act.dma_start(params[ROW_H0:ROWS, :], a["state_lru_h"][0]).then_inc(S["params_in"], 16)
            act.wait_ge(S["bd_zero"], 2)
            for dst, name in ((wa_bd, "lru_wa"), (wi_bd, "lru_wi")):
                for odd in range(2):
                    act.dma_start(dst[64 * odd:64 * odd + 64, :, 64 * odd:64 * odd + 64],
                                  a[name][0].rearrange("(j two) i o -> two i j o", two=2)[odd])\
                        .then_inc(S["gatew_in"], 16)
            act.dma_start(router_w[:, :, :], a["router_w"][0].rearrange("(c p) e -> p c e", p=P))\
                .then_inc(S["router_in"], 16)
            act.dma_start(router_b[:, :], a["router_b"].partition_broadcast(P).rearrange("p o n -> p (o n)"))\
                .then_inc(S["router_in"], 16)
            for v, name in ((ln_g, "ln1_g"), (ln_b, "ln1_b")):
                act.dma_start(v[:, :], a[name].partition_broadcast(P).rearrange("p o n -> p (o n)"))\
                    .then_inc(S["ln1_in"], 16)
            for t in range(2):
                act.wait_ge(S["xt_psum"], t + 1)
                s_.copy(xT[:, 4:8, t * P:(t + 1) * P], bank[2 * t + 1][:, :].rearrange("p (c n) -> p c n", c=4))\
                    .then_inc(S["xt_act"], 1)
            act.wait_ge(S["lam_abs"], 1)
            s_.activation(small[:, 1, :], small[:, 0, :], ACT.Exp, scale=-1.0).then_inc(S["lam_exp"], 1)
            act.wait_ge(S["lam_w"], 1)
            s_.activation(small[:, 3, :], small[:, 2, :], ACT.Ln).then_inc(S["lam_ln"], 1)
            act.wait_ge(S["pads_ok"], 2)
            for j in range(CT):
                act.wait_ge(S["proj_done"], j + 1)
                s_.copy(xl_pad[:, j, HIST:S0], bank[j][:, 0:SEQ])
                s_.copy(xl_pad[:, j, S0:FW].rearrange("p (b s) -> p b s", s=SEG)[:, :, HIST:SEG],
                        bank[j][:, SEQ:T].rearrange("p (b s) -> p b s", s=DS)).then_inc(S["xl_ok"], 1)
            for j in range(CT):
                act.wait_ge(S["proj_done"], CT + j + 1)
                s_.copy(gl[:, j, :], bank[j][:, 0:T]).then_inc(S["gl_ok"], 1)
            def gate_sigmoids(j):
                act.wait_ge(S["gates_psum"], j + 1)
                s_.activation(decay[:, j, :], bank[4][:, 0:OW], ACT.Sigmoid, bias=chan[:, j, ROW_BA:ROW_BA + 1])
                s_.activation(drive[:, j, :], bank[5][:, 0:OW], ACT.Sigmoid, bias=chan[:, j, ROW_BI:ROW_BI + 1])\
                    .then_inc(S["sig_ok"], 1)

            for j in range(CT):
                act.wait_ge(S["proj_done"], 2 * CT + j + 1)
                s_.copy(gate_c[:, j, :], bank[j][:, 0:T]).then_inc(S["c_ok"], 1)
                gate_sigmoids(j)
            act.wait_ge(S["gelu_in"], 1)
            s_.activation(tmp[:, :, 0:T], tmp[:, :, 0:T], ACT.Tanh, scale=GELU_B).then_inc(S["gelu_t"], 1)
            act.wait_ge(S["lam_ok"], 1)
            act.wait_ge(S["sig_ok"], CT)
            for j in range(CT):
                settle(s_.activation(mult[:, j, :], decay[:, j, :], ACT.Tanh, scale=lam8[:, 1, j:j + 1]))
                s_.activation(decay[:, j, :], decay[:, j, :], ACT.Exp, scale=lam8[:, 0, j:j + 1])\
                    .then_inc(S["ath_ok"], 1)
            act.wait_ge(S["one_m"], 1)
            s_.activation(mult, mult, ACT.Sqrt).then_inc(S["mult_ok"], 1)
            for grp in "ba":
                act.wait_ge(S[f"rms{grp}_in"], 1)
                s_.activation(rms, rms, ACT.Sqrt).then_inc(S[f"rms{grp}_ok"], 1)
            act.wait_ge(S["states_psum"], 1)
            s_.copy(states_out, bank[6][0:OUTS, :]).then_inc(S["states_sb"], 1)
            act.wait_ge(S["states_sb"], 1)
            for name, col, n in (("prompt_conv_a", OUT_PA, 2), ("prompt_conv_b", OUT_PB, 3), ("prompt_lru_h", OUT_PH, 1),
                                 ("sample_conv_a", OUT_SA, 16), ("sample_conv_b", OUT_SB, 24),
                                 ("sample_lru_h", OUT_SH, 8)):
                dst = a[name][0]
                if "conv" in name:
                    dst = dst.rearrange("b k c -> (b k) c")
                act.dma_start(dst, states_out[col:col + n, :]).then_inc(S["states_dma"], 16)
            for t, (t0, n) in enumerate(TILES):
                act.wait_ge(S["var_ok"], t + 1)
                s_.activation(rstd[0:n, t:t + 1], rstd[0:n, t:t + 1], ACT.Sqrt).then_inc(S["rstd_ok"], 1)
                act.wait_ge(S["shift_ok"], t + 1)
                s_.activation(x[0:n, t, :], x[0:n, t, :], ACT.Identity, bias=shift[0:n, t:t + 1],
                              scale=rstd[0:n, t:t + 1]).then_inc(S["norm_ok"], 1)
                if t:
                    x1_side(act, s_, t - 1)
            x1_side(act, s_, 2)
            for t, (t0, n) in enumerate(TILES):
                act.wait_ge(S["top_ok"], t + 1)
                s_.activation(gates[0:n, t, :], top_v[0:n, t, 0:TOPK], ACT.Exp, bias=gsum[0:n, t:t + 1],
                              accum_out=gsum[0:n, 3 + t:4 + t]).then_inc(S["exp_ok"], 1)
            act.wait_ge(S["xu_psum"], 1)
            s_.copy(xTu, bank[3][:, :]).then_inc(S["xu_ok"], 1)

            act.wait_ge(S["tab_ok"], 1)
            n_unit = act.value_load(unit_info[0:1, TABW:TABW + 1], min_val=NE, max_val=MAXU)
            with act.Fori(0, n_unit) as u:
                act.wait_ge(S["gate_free"], u + 2)
                s_.activation(sig, g_min, ACT.Sigmoid, scale=SWISH).then_inc(S["sig_done"], 1)
                act.wait_ge(S["xu_psum"], u + 2)
                s_.copy(xTu, bank[3][:, :]).then_inc(S["xu_ok"], 1)
                act.wait_ge(S["hu_psum"], u + 1)
                s_.copy(hTu, bank[4][:, :]).then_inc(S["hu_ok"], 1)
                act.wait_ge(S["y_done"], u + 1)
                act.wait_ge(S["acc_written"], u * 16 + 48)
                s_.activation(y_rows, bank[2][:, :], ACT.Copy, scale=unit_gate[:, bass.ds(u, 1)])\
                    .then_inc(S["y_ok"], 1)

            for t, (t0, n) in enumerate(TILES):
                act.wait_ge(S["ln2_var"], 2 * t + 1)
                s_.activation(rstd[0:n, t:t + 1], rstd[0:n, t:t + 1], ACT.Sqrt).then_inc(S["ln2_rstd"], 1)
                act.wait_ge(S["ln2_var"], 2 * t + 2)
                s_.activation(final[0:n, t, :], final[0:n, t, :], ACT.Identity, bias=shift[0:n, t:t + 1],
                              scale=rstd[0:n, t:t + 1]).then_inc(S["ln2_norm"], 1)

        @block.vector
        def _(dve):
            v = nc.vector
            step = [0]

            def settle(ins):
                step[0] += 1
                ins.then_inc(S["dve_step"], 1)
                dve.wait_ge(S["dve_step"], step[0])

            for t in range(3):
                dve.wait_ge(S["xt_psum"], t + 1)
                src = bank[2 * t][:, :]
                if t < 2:
                    v.tensor_copy(xT[:, 0:4, t * P:(t + 1) * P], src.rearrange("p (c n) -> p c n", c=4))\
                        .then_inc(S["xt_dve"], 1)
                else:
                    v.tensor_copy(xT[:, :, 2 * P:T], src.rearrange("p (c n) -> p c n", c=CH))\
                        .then_inc(S["xt_dve"], 1)
            dve.wait_ge(S["chan_psum"], 1)
            v.tensor_copy(chan[:, :, 0:ROWS], bank[6][:, 0:CT * 64].rearrange("p (c n) -> p c n", c=CT)[:, :, 0:ROWS])\
                .then_inc(S["chan_ok"], 1)
            dve.wait_ge(S["chan_ok"], 1)
            lam = chan[:, :, ROW_LAM]
            ab, q, w, lnw, d, rec, res, extra = (small[:, i, :] for i in range(8))
            v.scalar_tensor_tensor(ab, lam, -1.0, lam, ALU.mult, ALU.max).then_inc(S["lam_abs"], 1)
            dve.wait_ge(S["lam_exp"], 1)
            v.tensor_scalar(w, q, 1.0, None, ALU.add).then_inc(S["lam_w"], 1)
            dve.wait_ge(S["lam_w"], 1)
            settle(v.tensor_scalar(d, w, -1.0, None, ALU.add))
            settle(v.tensor_scalar(rec, d, 1e-30, None, ALU.max))
            settle(v.reciprocal(rec, rec))
            settle(v.tensor_tensor(rec, rec, q, ALU.mult))
            settle(v.tensor_scalar(extra, d, 0.0, None, ALU.is_equal))
            settle(v.tensor_tensor(extra, extra, q, ALU.mult))
            dve.wait_ge(S["lam_ln"], 1)
            settle(v.tensor_tensor(res, lnw, rec, ALU.mult))
            settle(v.tensor_tensor(res, res, extra, ALU.add))
            settle(v.tensor_scalar(extra, lam, -1.0, 0.0, ALU.mult, ALU.max))
            settle(v.tensor_tensor(res, res, extra, ALU.add))
            v.tensor_scalar(lam8[:, 0, :], res, -LRU_C, None, ALU.mult)
            v.tensor_scalar(lam8[:, 1, :], res, LRU_C, None, ALU.mult).then_inc(S["lam_ok"], 1)

            dve.wait_ge(S["hist_ok"], CT)
            for j in range(CT):
                dve.wait_ge(S["xl_ok"], j + 1)
                settle(v.tensor_scalar(xc[:, j, :], xl_pad[:, j, 0:OW], chan[:, j, ROW_WB:ROW_WB + 1],
                                       chan[:, j, ROW_CB:ROW_CB + 1], ALU.mult, ALU.add))
                for k in range(1, 4):
                    last = v.scalar_tensor_tensor(xc[:, j, :], xl_pad[:, j, k:k + OW],
                                                  chan[:, j, ROW_WB + k:ROW_WB + k + 1], xc[:, j, :],
                                                  ALU.mult, ALU.add)
                    if k < 3:
                        settle(last)
                last.then_inc(S["xc_ok"], 1)
            arg = tmp[:, :, 0:T]
            dve.wait_ge(S["gl_ok"], CT)
            settle(v.tensor_tensor(arg, gl, gl, ALU.mult))
            settle(v.tensor_scalar(arg, arg, GELU_A, 1.0, ALU.mult, ALU.add))
            v.tensor_tensor(arg, arg, gl, ALU.mult).then_inc(S["gelu_in"], 1)
            dve.wait_ge(S["gelu_t"], 1)
            settle(v.scalar_tensor_tensor(gl, arg, 1.0, gl, ALU.add, ALU.mult))

            def masked_v(j):
                dve.wait_ge(S["proj_done"], 3 * CT + j + 1)
                v.tensor_tensor(cv_pad[:, j, HIST:S0], bank[j][:, 0:SEQ], gate_c[:, j, 0:SEQ], ALU.mult)\
                    .then_inc(S["cv_ok"], 1)
                v.tensor_tensor(cv_pad[:, j, S0:FW].rearrange("p (b s) -> p b s", s=SEG)[:, :, HIST:SEG],
                                bank[j][:, SEQ:T].rearrange("p (b s) -> p b s", s=DS),
                                gate_c[:, j, SEQ:T].rearrange("p (b s) -> p b s", s=DS), ALU.mult)\
                    .then_inc(S["cv_ok"], 1)

            dve.wait_ge(S["ath_ok"], CT)
            settle(v.tensor_tensor(tmp, decay, decay, ALU.mult))
            v.scalar_tensor_tensor(mult, tmp, 1.0, mult, ALU.add, ALU.mult).then_inc(S["one_m"], 1)
            settle(v.tensor_tensor(drive, drive, xc, ALU.mult))
            dve.wait_ge(S["c_ok"], CT)
            masked_v(0)
            dve.wait_ge(S["mult_ok"], 1)
            settle(v.tensor_tensor(drive, drive, mult, ALU.mult))
            for j in range(CT):
                v.memset(decay[:, j, 0:1], 0.0)
                v.memset(decay[:, j, S0 - 1:OW:SEG], 0.0)
                last = v.tensor_copy(drive[:, j, S0 - 1:OW:SEG], chan[:, j, ROW_H0:ROW_H0 + NB])
            settle(last)
            h = xc.rearrange("p c w -> p (c w)")
            v.tensor_tensor_scan(h, decay.rearrange("p c w -> p (c w)"), drive.rearrange("p c w -> p (c w)"),
                                 0.0, ALU.mult, ALU.add).then_inc(S["h_ok"], 1)
            masked_v(1)
            dve.wait_ge(S["h_ok"], 1)
            settle(v.scalar_tensor_tensor(mixT[:, CT:CH, 0:SEQ], gl[:, :, 0:SEQ], 0.5, xc[:, :, 0:SEQ],
                                          ALU.mult, ALU.mult))
            for j in range(CT):
                last = v.scalar_tensor_tensor(
                    mixT[:, CT + j, SEQ:T].rearrange("p (b s) -> p b s", s=DS),
                    gl[:, j, SEQ:T].rearrange("p (b s) -> p b s", s=DS), 0.5,
                    sample_cols(xc, j), ALU.mult, ALU.mult)
            settle(last)
            sq = tmp[:, :, 0:T]
            v.tensor_tensor(sq, mixT[:, CT:CH, :], mixT[:, CT:CH, :], ALU.mult).then_inc(S["sqb_ok"], 1)

            def conv_a_tile(j):
                dve.wait_ge(S["cv_ok"], 2 * (j + 1))
                settle(v.tensor_scalar(conv_a[:, j, :], cv_pad[:, j, 1:1 + OW], chan[:, j, ROW_WA:ROW_WA + 1],
                                       None, ALU.mult))
                for k in range(1, 3):
                    settle(v.scalar_tensor_tensor(conv_a[:, j, :], cv_pad[:, j, 1 + k:1 + k + OW],
                                                  chan[:, j, ROW_WA + k:ROW_WA + k + 1], conv_a[:, j, :],
                                                  ALU.mult, ALU.add))

            def gated_a(j):
                dve.wait_ge(S["proj_done"], 4 * CT + j + 1)
                v.tensor_tensor(mixT[:, j, 0:SEQ], bank[j][:, 0:SEQ], conv_a[:, j, 0:SEQ], ALU.mult)
                v.tensor_tensor(mixT[:, j, SEQ:T].rearrange("p (b s) -> p b s", s=DS),
                                bank[j][:, SEQ:T].rearrange("p (b s) -> p b s", s=DS), sample_cols(conv_a, j),
                                ALU.mult).then_inc(S["bank_dve"], 1)

            masked_v(2)
            masked_v(3)
            for j in range(CT):
                conv_a_tile(j)

            def inv_rms_in(b, s):
                settle(v.tensor_scalar(rms, b[:, 0:T], 1.0 / CW, RMS_EPS, ALU.mult, ALU.add))
                v.reciprocal(rms, rms).then_inc(S[s], 1)

            def normed(grp, row, done, s):
                dve.wait_ge(S[done], 1)
                for j in range(CT):
                    last = v.scalar_tensor_tensor(mixT[:, grp * CT + j, :], mixT[:, grp * CT + j, :],
                                                  chan[:, j, row:row + 1], rms, ALU.mult, ALU.mult)
                last.then_inc(S[s], 1)

            gated_a(0)
            gated_a(1)
            dve.wait_ge(S["rmsb_psum"], 1)
            inv_rms_in(bank[6], "rmsb_in")
            normed(1, ROW_GB, "rmsb_ok", "yb_ok")
            gated_a(2)
            gated_a(3)
            dve.wait_ge(S["bank_dve"], CT)
            v.tensor_tensor(sq, mixT[:, 0:CT, :], mixT[:, 0:CT, :], ALU.mult).then_inc(S["sqa_ok"], 1)
            dve.wait_ge(S["rmsa_psum"], 1)
            dve.wait_ge(S["yb_ok"], 1)
            inv_rms_in(bank[7], "rmsa_in")
            normed(0, ROW_GA, "rmsa_ok", "ya_ok")

            def moments(src, t, n, s):
                v.bn_stats(stats[0:n, t, 0:6], src[0:n, t, 0:512])
                settle(v.bn_stats(stats[0:n, t, 6:12], src[0:n, t, 512:1024]))
                settle(v.bn_aggr(mean_var[0:n, t, :], stats[0:n, t, :].rearrange("p (a b) -> p a b", b=6)))
                settle(v.tensor_scalar(rstd[0:n, t:t + 1], mean_var[0:n, t, 1:2], LN_EPS, None, ALU.add))
                v.reciprocal(rstd[0:n, t:t + 1], rstd[0:n, t:t + 1]).then_inc(S[s], 1)

            def offset(t, n, s):
                v.scalar_tensor_tensor(shift[0:n, t:t + 1], mean_var[0:n, t, 0:1], -1.0, rstd[0:n, t:t + 1],
                                       ALU.mult, ALU.mult).then_inc(S[s], 1)

            def affine(dst, t, n, s):
                settle(v.tensor_tensor(dst[0:n, t, :], dst[0:n, t, :], ln_g[0:n, :], ALU.mult))
                v.tensor_tensor(dst[0:n, t, :], dst[0:n, t, :], ln_b[0:n, :], ALU.add).then_inc(S[s], 1)

            dve.wait_ge(S["ln1_in"], 32)

            def residual(t):
                n = TILES[t][1]
                dve.wait_ge(S["out_psum"], t + 1)
                for h_ in range(2):
                    last = v.scalar_tensor_tensor(x[0:n, t, h_ * 512:(h_ + 1) * 512],
                                                  x[0:n, t, h_ * 512:(h_ + 1) * 512], ALPHA,
                                                  bank[2 * t + h_][0:n, :], ALU.mult, ALU.add)
                settle(last)
                moments(x, t, n, "var_ok")

            def finish_norm(t):
                n = TILES[t][1]
                dve.wait_ge(S["rstd_ok"], t + 1)
                offset(t, n, "shift_ok")
                dve.wait_ge(S["norm_ok"], t + 1)
                affine(x, t, n, "x1_ok")

            def x1t(t):
                dve.wait_ge(S["x1t_psum"], t + 1)
                if t < 2:
                    v.tensor_copy(xT[:, 0:4, t * P:(t + 1) * P],
                                  bank[(6, 2)[t]][:, :].rearrange("p (c n) -> p c n", c=4)).then_inc(S["x1t_dve"], 1)
                else:
                    v.tensor_copy(xT[:, :, 2 * P:T], bank[4][:, :].rearrange("p (c n) -> p c n", c=CH))\
                        .then_inc(S["x1t_dve"], 1)

            residual(0)
            finish_norm(0)
            residual(1)
            finish_norm(1)
            x1t(0)
            residual(2)
            finish_norm(2)
            x1t(1)
            x1t(2)

            dve.wait_ge(S["router_in"], 32)
            settle(v.memset(zeros_e, 0.0))
            for t, (t0, n) in enumerate(TILES):
                dve.wait_ge(S["logit_psum"], t + 1)
                settle(v.tensor_tensor(logits[0:n, t, :], bank[(0, 1, 5)[t]][0:n, 0:NE], router_b[0:n, :], ALU.add))
                settle(v.max(top_v[0:n, t, :], logits[0:n, t, :]))
                v.tensor_scalar(gsum[0:n, t:t + 1], top_v[0:n, t, 0:1], -1.0, None, ALU.mult).then_inc(S["top_ok"], 1)
                settle(v.max_index(top_i[0:n, t, :].bitcast(u32), top_v[0:n, t, :], logits[0:n, t, :]))
                settle(v.tensor_copy(top_f[0:n, t, :], top_i[0:n, t, 0:TOPK].bitcast(u32)))
                hot = onehot[0:n, t, :].rearrange("p (k e) -> p k e", e=NE)
                settle(v.tensor_tensor(hot, iota_e[0:n, :].unsqueeze(1).to_broadcast([n, TOPK, NE]),
                                       top_f[0:n, t, :].unsqueeze(2).to_broadcast([n, TOPK, NE]), ALU.is_equal))
                settle(v.reduce_sum(chosen_f[0:n, t, :], hot.rearrange("p k e -> p e k"), AX.X))
                v.tensor_copy(chosen[0:n, t, :], chosen_f[0:n, t, :]).then_inc(S["chosen_ok"], 1)
            for t, (t0, n) in enumerate(TILES):
                dve.wait_ge(S["exp_ok"], t + 1)
                settle(v.reciprocal(gsum[0:n, 3 + t:4 + t], gsum[0:n, 3 + t:4 + t]))
                settle(v.tensor_scalar(gates[0:n, t, :], gates[0:n, t, :], gsum[0:n, 3 + t:4 + t], None, ALU.mult))
            dve.wait_ge(S["rank_psum"], 1)
            settle(v.tensor_copy(counts, bank[6][:, 3 * NE:4 * NE]))
            settle(v.tensor_scalar(n_units, counts, float(UT), 1.0, ALU.is_gt, ALU.add))
            for k in range(2, T // UT):
                settle(v.scalar_tensor_tensor(n_units, counts, float(k * UT), n_units, ALU.is_gt, ALU.add))
            settle(v.tensor_tensor_scan(ends, n_units, zeros_e, 0.0, ALU.add, ALU.add))
            settle(v.tensor_tensor(first, ends, n_units, ALU.subtract))
            settle(v.tensor_scalar(first, first, float(UT), None, ALU.mult))
            for t, (t0, n) in enumerate(TILES):
                settle(v.tensor_tensor(pos[0:n, t, :], bank[6][0:n, t * NE:(t + 1) * NE], first[0:n, :], ALU.add))
                picks = picked[0:n, t, :].rearrange("p (k e) -> p k e", e=NE)
                settle(v.tensor_tensor(picks, onehot[0:n, t, :].rearrange("p (k e) -> p k e", e=NE),
                                       pos[0:n, t, :].unsqueeze(1).to_broadcast([n, TOPK, NE]), ALU.mult))
                settle(v.reduce_sum(place[0:n, t, :], picks, AX.X))
                settle(v.tensor_copy(place_i[0:n, t, :], place[0:n, t, :]))
                v.tensor_scalar(slot_i[0:n, t, :], place_i[0:n, t, :], UT - 1, None, ALU.bitwise_and)
                settle(v.tensor_scalar(unit_i[0:n, t, :], place_i[0:n, t, :], UT.bit_length() - 1, None,
                                       ALU.logical_shift_right))
                v.tensor_copy(slot_f[0:n, t, :], slot_i[0:n, t, :])
                settle(v.tensor_copy(unit_f[0:n, t, :], unit_i[0:n, t, :]))
                for k in range(TOPK):
                    i = t * TOPK + k
                    v.tensor_scalar(slot_hot[0:n, i, :], iota_s[0:n, :], slot_f[0:n, t, k:k + 1], None, ALU.is_equal)
                    v.tensor_scalar(unit_val[0:n, i, 0:TABW], iota_u[0:n, :], unit_f[0:n, t, k:k + 1],
                                    tok_val[0:n, t:t + 1], ALU.is_equal, ALU.mult)
                    v.tensor_scalar(unit_val[0:n, i, TABW:2 * TABW], iota_u[0:n, :], unit_f[0:n, t, k:k + 1],
                                    gates[0:n, t, k:k + 1], ALU.is_equal, ALU.mult).then_inc(S["hot_ok"], 1)
            settle(v.tensor_tensor(before, ends[0:1, :].unsqueeze(1).to_broadcast([1, TABW, NE]),
                                   iota_u[0:1, :].unsqueeze(2).to_broadcast([1, TABW, NE]), ALU.is_le))
            settle(v.reduce_sum(row_f[0:1, 0, :], before, AX.X))
            settle(v.tensor_scalar(unit_info[0:1, 0:TABW], row_f[0:1, 0, :], float(NE - 1), None, ALU.min))
            settle(v.tensor_copy(unit_info[0:1, TABW:TABW + 1], ends[0:1, NE - 1:NE]))
            dve.wait_ge(S["tab_psum"], 1)
            settle(v.tensor_copy(unit_gate[:, :], bank[7][:, TABW:2 * TABW]))
            settle(v.tensor_scalar(row_f[:, 0, :], bank[7][:, 0:TABW], 0.0, EMPTY, ALU.is_equal, ALU.mult))
            settle(v.tensor_tensor(row_f[:, 1, :], bank[7][:, 0:TABW], row_f[:, 0, :], ALU.add))
            settle(v.tensor_scalar(row_f[:, 1, :], row_f[:, 1, :], -1.0, 2.0, ALU.add, ALU.mult))
            v.tensor_scalar(unit_rows[:, :], row_f[:, 1, :], half_col[:, 0:1], None, ALU.add)\
                .then_inc(S["tab_ok"], 1)

            dve.wait_ge(S["tab_ok"], 1)
            dve.sem_inc(S["gate_free"], 1)
            dve.sem_inc(S["up_free"], 1)
            dve.sem_inc(S["y_ok"], 1)
            n_unit = dve.value_load(unit_info[0:1, TABW:TABW + 1], min_val=NE, max_val=MAXU)
            with dve.Fori(0, n_unit) as u:
                dve.wait_ge(S["gate_done"], u + 1)
                v.tensor_scalar(g_min, bank[0][:, :], LIMIT, None, ALU.min).then_inc(S["gate_free"], 1)
                dve.wait_ge(S["sig_done"], u + 1)
                v.tensor_tensor(g_min, g_min, sig, ALU.mult).then_inc(S["glu_ok"], 1)
                dve.wait_ge(S["up_done"], u + 1)
                v.tensor_scalar(up_clip, bank[1][:, :], LIMIT, -LIMIT, ALU.min, ALU.max).then_inc(S["up_free"], 1)
                dve.wait_ge(S["up_free"], u + 2)
                dve.wait_ge(S["glu_ok"], u + 1)
                v.scalar_tensor_tensor(hid, up_clip, 1.0, g_min, ALU.add, ALU.mult).then_inc(S["hid_ok"], 1)

            dve.wait_ge(S["ln2_in"], 32)

            def residual2(t):
                n = TILES[t][1]
                moments(final, t, n, "ln2_var")
                dve.wait_ge(S["ln2_rstd"], t + 1)
                offset(t, n, "ln2_var")

            dve.wait_ge(S["acc_in"], 48)
            residual2(0)
            for t, (t0, n) in enumerate(TILES):
                if t < 2:
                    residual2(t + 1)
                dve.wait_ge(S["ln2_norm"], t + 1)
                affine(final, t, n, "ln2_ok")

        @block.tensor
        def _(pe):
            mm = nc.tensor.matmul
            pe.wait_ge(S["ident_ok"], 1)
            pe.wait_ge(S["x_in"], 48)
            for t, (t0, n) in enumerate(TILES):
                for c in range(CH):
                    b, col = (2 * t + c // 4, (c % 4) * P) if t < 2 else (4, c * n)
                    last = nc.tensor.transpose(bank[b][:, col:col + n], x[0:n, t, c * P:(c + 1) * P],
                                               ident[0:n, 0:n])
                last.then_inc(S["xt_psum"], 1)
            pe.wait_ge(S["params_in"], 16 * 11)
            for j in range(CT):
                last = nc.tensor.transpose(bank[6][:, j * 64:j * 64 + ROWS], params[:, j * P:(j + 1) * P],
                                           ident[0:ROWS, 0:ROWS])
            last.then_inc(S["chan_psum"], 1)
            pe.wait_ge(S["xt_dve"], 3)
            pe.wait_ge(S["xt_act"], 2)

            def gate_products(j):
                pe.wait_ge(S["xc_ok"], j + 1)
                if j:
                    pe.wait_ge(S["sig_ok"], j)
                mm(bank[4][:, 0:OW], wa_bd[:, j, :], xc[:, j, :], start=True, stop=True)
                mm(bank[5][:, 0:OW], wi_bd[:, j, :], xc[:, j, :], start=True, stop=True)\
                    .then_inc(S["gates_psum"], 1)

            def sum_squares(b, ok, s):
                pe.wait_ge(S[ok], 1)
                for j in range(CT):
                    last = mm(bank[b][:, 0:T], ones[:, :], tmp[:, j, 0:T], start=j == 0, stop=j == CT - 1)
                last.then_inc(S[s], 1)

            freed = {1: ("xl_ok", 1), 2: ("gl_ok", 1), 3: ("c_ok", 1), 4: ("cv_ok", 2)}
            seen = [0] * NSLOT
            pe.wait_ge(S["gatew_in"], 64)
            pe.wait_ge(S["consts_ok"], 1)
            for gi, (g, s) in enumerate(IN_GROUPS):
                seen[s] += 1
                pe.wait_ge(slot_loaded[s], 16 * seen[s])
                w = ring[:, s, :].rearrange("p (c n) -> p c n", n=CW)
                for j in range(CT):
                    if gi:
                        name, per = freed[gi]
                        pe.wait_ge(S[name], per * (j + 1))
                    for c in range(CH):
                        last = mm(bank[j][:, 0:T], w[:, c, j * P:(j + 1) * P], xT[:, c, :],
                                  start=c == 0, stop=c == CH - 1)
                    last.then_inc(S["proj_done"], 1)
                    if gi == 2:
                        gate_products(j)
                    if gi == 4 and j == 1:
                        sum_squares(6, "sqb_ok", "rmsb_psum")
            sum_squares(7, "sqa_ok", "rmsa_psum")
            for grp, s, ok in ((1, 5, "yb_ok"), (0, 3, "ya_ok")):
                seen[s] += 1
                pe.wait_ge(S[ok], 1)
                pe.wait_ge(slot_loaded[s], 16 * seen[s])
                if grp:
                    pe.wait_ge(S["bank_dve"], CT)
                for t, (t0, n) in enumerate(TILES):
                    for h_ in range(2):
                        for c in range(CT):
                            last = mm(bank[2 * t + h_][0:n, :], mixT[:, grp * CT + c, t0:t0 + n],
                                      slot(s)[:, c, h_ * 512:(h_ + 1) * 512],
                                      start=grp == 1 and c == 0, stop=grp == 0 and c == CT - 1)
                    if grp == 0:
                        last.then_inc(S["out_psum"], 1)
                if grp:
                    last.then_inc(S["lru_rows_used"], 1)
            pe.wait_ge(S["states_ok"], 1)
            pe.wait_ge(S["rmsb_in"], 1)
            for j in range(CT):
                last = nc.tensor.transpose(bank[6][0:OUTS, j * P:(j + 1) * P], states[:, j, 0:OUTS], ident[:, :])
            last.then_inc(S["states_psum"], 1)
            pe.wait_ge(S["states_sb"], 1)
            pe.wait_ge(S["rmsa_in"], 1)
            pe.wait_ge(S["router_in"], 32)
            for t, (t0, n) in enumerate(TILES):
                pe.wait_ge(S["x1_ok"], t + 1)
                for c in range(CH):
                    b, col = ((6, 2)[t] + c // 4, (c % 4) * P) if t < 2 else (4, c * n)
                    last = nc.tensor.transpose(bank[b][:, col:col + n], x[0:n, t, c * P:(c + 1) * P],
                                               ident[0:n, 0:n])
                last.then_inc(S["x1t_psum"], 1)
                pe.wait_ge(S["x1t_dve"], t + 1)
                pe.wait_ge(S["x1t_act"], min(t + 1, 2))
                for c in range(CH):
                    last = mm(bank[(0, 1, 5)[t]][0:n, 0:NE], xT[:, c, t0:t0 + n], router_w[:, c, :],
                              start=c == 0, stop=c == CH - 1)
                last.then_inc(S["logit_psum"], 1)
            pe.wait_ge(S["chosen_ok"], 3)
            for t, (t0, n) in enumerate(TILES):
                for t2 in range(t):
                    mm(bank[6][0:n, t * NE:(t + 1) * NE], ones_bf[:, 0:n], chosen[:, t2, :],
                       start=t2 == 0, stop=False)
                mm(bank[6][0:n, t * NE:(t + 1) * NE], earlier_bf[0:n, 0:n], chosen[0:n, t, :],
                   start=t == 0, stop=True)
            for t, (t0, n) in enumerate(TILES):
                last = mm(bank[6][:, 3 * NE:4 * NE], ones_bf[0:n, :], chosen[0:n, t, :],
                          start=t == 0, stop=t == 2)
            last.then_inc(S["rank_psum"], 1)
            for t, (t0, n) in enumerate(TILES):
                for k in range(TOPK):
                    i = t * TOPK + k
                    pe.wait_ge(S["hot_ok"], i + 1)
                    last = mm(bank[7][:, 0:2 * TABW], slot_hot[0:n, i, :], unit_val[0:n, i, :],
                              start=i == 0, stop=i == 3 * TOPK - 1)
            last.then_inc(S["tab_psum"], 1)

            def transposed(b, src, s):
                for c in range(4):
                    last = nc.tensor.transpose(bank[b][:, c * P:(c + 1) * P], src[:, c * P:(c + 1) * P], ident[:, :])
                last.then_inc(S[s], 1)

            pe.wait_ge(S["gathered"], 16)
            transposed(3, x_rows, "xu_psum")

            pe.wait_ge(S["tab_ok"], 1)
            n_unit = pe.value_load(unit_info[0:1, TABW:TABW + 1], min_val=NE, max_val=MAXU)
            with pe.Fori(0, n_unit) as u:
                def product(b, m, left, s):
                    for hf in range(2):
                        pe.wait_ge(slot_loaded[2 * m + hf], u * 16 + 16 * (PRIOR[2 * m + hf] + 1))
                        w = slot(2 * m + hf)
                        for c in range(4):
                            lhsT = left[:, c * P + hf * UT:c * P + hf * UT + UT]
                            end = hf == 1 and c == 3
                            for side in range(2):
                                last = mm(bank[b][side * UT:(side + 1) * UT, :], lhsT,
                                          w[:, c, side * HALF:(side + 1) * HALF], start=False, stop=end,
                                          skip_group_check=True)
                        if hf == 0:
                            last.then_inc(half_used[m], 1)
                    last.then_inc(S[s], 1)

                def biased(b, m):
                    return mm(bank[b][:, :], half_sel[:, :], bias_rows[:, m, :], start=True, stop=False,
                              skip_group_check=True)

                pe.wait_ge(S["xu_ok"], u + 1)
                pe.wait_ge(S["bias_in"], u * 48 + 48)
                pe.wait_ge(S["gate_free"], u + 1)
                biased(0, 0)
                product(0, 0, xTu, "gate_done")
                pe.wait_ge(S["up_free"], u + 1)
                biased(1, 1)
                product(1, 1, xTu, "up_done")
                pe.wait_ge(S["gathered"], u * 16 + 32)
                transposed(3, x_rows, "xu_psum")
                pe.wait_ge(S["y_ok"], u + 1)
                biased(2, 2).then_inc(S["bias_used"], 1)
                pe.wait_ge(S["hid_ok"], u + 1)
                transposed(4, hid, "hu_psum")
                pe.wait_ge(S["hu_ok"], u + 1)
                product(2, 2, hTu, "y_done")


_INS = ["x_prompt", "x_sample", "state_conv_a", "state_conv_b", "state_lru_h", "w_in", "conv_a_w", "conv_b_w",
        "conv_b_b", "lru_wa", "lru_ba", "lru_wi", "lru_bi", "lru_lambda", "gn_a", "gn_b", "w_out", "ln1_g", "ln1_b",
        "router_w", "router_b", "exp_w_gate", "exp_b_gate", "exp_w_up", "exp_b_up", "exp_w_down", "exp_b_down",
        "ln2_g", "ln2_b"]
_OUTS = [("y_prompt", (1, SEQ, D)), ("y_sample", (NB, DS, D)), ("prompt_conv_a", (1, 1, 2, CW)),
         ("prompt_conv_b", (1, 1, 3, CW)), ("prompt_lru_h", (1, 1, CW)), ("sample_conv_a", (1, NB, 2, CW)),
         ("sample_conv_b", (1, NB, 3, CW)), ("sample_lru_h", (1, NB, CW))]


def kernel(**inputs):
    import numpy as np
    import concourse.bacc as bacc
    from concourse.bass_utils import run_bass_kernel_spmd

    nc = bacc.Bacc("TRN2", target_bir_lowering=False, num_devices=1)
    arrays, args = {}, {}
    for name in _INS:
        v = np.ascontiguousarray(inputs[name])
        arrays[f"in_{name}"] = v
        args[name] = nc.dram_tensor(f"in_{name}", v.shape, mybir.dt.from_np(v.dtype), kind="ExternalInput").ap()
    for name, shape in _OUTS:
        args[name] = nc.dram_tensor(f"out_{name}", shape, mybir.dt.float32, kind="ExternalOutput").ap()
    hybrid_layer(nc, args)
    r = run_bass_kernel_spmd(nc, [arrays], core_ids=[0])
    return tuple(r.results[0][f"out_{name}"] for name, _ in _OUTS)
```

```python
import math
from contextlib import ExitStack

import concourse.bass as bass
from concourse import mybir

P = 128
D = 1024
CH = D // P
SEQ = 256
NB, DS = 8, 8
T = SEQ + NB * DS
TILES = [(0, 128), (128, 128), (256, 64)]
CW = 512
CT = CW // P
HIST = 3
SEG = HIST + DS
S0 = HIST + SEQ
FW = S0 + NB * SEG
OW = FW - HIST
NE, TOPK = 32, 4
UT = 64
MAXU = NE + T * TOPK // UT
TABW = MAXU + 1
HALF = D // 2
SLOTW = 4 * D
NSLOT = 6
EMPTY = 65536.0
ALPHA = 2.0 ** 0.25
LIMIT, SWISH = 7.0, 1.702
LN_EPS, RMS_EPS = 1e-5, 1e-6
LRU_C = 8.0
GELU_A, GELU_B = 0.044715, math.sqrt(2.0 / math.pi)

ROW_WA, ROW_WB, ROW_CB, ROW_BA, ROW_BI, ROW_LAM, ROW_GA, ROW_GB = 0, 3, 7, 8, 9, 10, 11, 12
ROW_SA, ROW_SB, ROW_H0, ROWS = 13, 29, 53, 61
OUT_PA, OUT_PB, OUT_PH, OUT_SA, OUT_SB, OUT_SH, OUTS = 0, 2, 5, 6, 22, 46, 54

IN_GROUPS = [(3, 3), (4, 4), (2, 5), (0, 3), (1, 4)]
LRU_BANKS = [(4, 5), (6, 1), (0, 0)]
CONV_BANKS = [(2, 3), (4, 5), (0, 0)]
LOGIT_BANKS = [1, 7, 3]
PRIOR = [0, 0, 0, 3, 2, 2]


def hybrid_layer(nc, a):
    fp32, bf16, i32, u32 = mybir.dt.float32, mybir.dt.bfloat16, mybir.dt.int32, mybir.dt.uint32
    ALU, ACT, AX = mybir.AluOpType, mybir.ActivationFunctionType, mybir.AxisListType
    with ExitStack() as ctx:
        def sb(name, shape, dt=fp32):
            return ctx.enter_context(nc.sbuf_tensor(name, shape, dt))

        def sem(name):
            return ctx.enter_context(nc.semaphore(name))

        ring = sb("ring", [P, NSLOT, SLOTW])
        x = sb("x", [P, 3, D])
        xT = sb("xT", [P, CH, T])
        ident = sb("ident", [P, P])
        ones = sb("ones", [P, P])
        ones_bf = sb("ones_bf", [P, P], bf16)
        earlier_bf = sb("earlier_bf", [P, P], bf16)
        half_sel = sb("half_sel", [2, P])
        half_off = sb("half_off", [P, 1])
        iota_i = sb("iota_i", [P, P], i32)
        iota_e = sb("iota_e", [P, NE])
        iota_u = sb("iota_u", [P, TABW])
        iota_s = sb("iota_s", [P, UT])
        tok_val = sb("tok_val", [P, 3])
        router_w = sb("router_w", [P, CH, NE])
        router_b = sb("router_b", [P, NE])
        ln_g = sb("ln_g", [P, D])
        ln_b = sb("ln_b", [P, D])
        stats = sb("stats", [P, 3, 12])
        mean_var = sb("mean_var", [P, 3, 2])
        rstd = sb("rstd", [P, 3])
        shift = sb("shift", [P, 3])
        unit_rows = sb("unit_rows", [P, TABW], i32)
        unit_gate = sb("unit_gate", [P, TABW])
        unit_expert = sb("unit_expert", [1, TABW], i32)
        units_through = sb("units_through", [1, NE], i32)
        rows_g = sb("rows_g", [P, 1], i32)
        rows_s = sb("rows_s", [P, 1], i32)

        AREA = 15600
        area = sb("area", [P, AREA])
        at = [0]

        def carve(parts, *dims, dt=fp32):
            n = math.prod(dims)
            v = area[0:parts, at[0]:at[0] + n]
            at[0] += n
            assert at[0] <= AREA, at[0]
            if dt != fp32:
                v = v.bitcast(dt)
            if len(dims) == 2:
                v = v.rearrange("p (a b) -> p a b", b=dims[1])
            elif len(dims) == 3:
                v = v.rearrange("p (a b c) -> p a b c", b=dims[1], c=dims[2])
            return v

        xl_pad = carve(P, CT, FW)
        cv_pad = carve(P, CT, FW)
        xc = carve(P, CT, OW)
        decay = carve(P, CT, OW)
        drive = carve(P, CT, OW)
        mult = carve(P, CT, OW)
        gate_c = carve(P, CT, T)
        gl = carve(P, CT, T)
        tmp = carve(P, CT, OW)
        conv_a = mult
        conv_gained = drive
        plain_a = decay
        params = carve(ROWS, CW)
        chan = carve(P, CT, 64)
        lam8 = carve(P, 2, CT)
        small = carve(P, 8, CT)
        wa_bd = carve(P, CT, P)
        wi_bd = carve(P, CT, P)
        rms = carve(P, 6)
        states = carve(P, CT, 64)
        states_out = carve(OUTS, CW)
        mixer_end = at[0]
        mixT = sb("mixT", [P, CH, T])
        at[0] = 0
        scaled = carve(P, 3, D)
        logits = carve(P, 3, NE)
        top_v = carve(P, 3, 8)
        top_i = carve(P, 3, 8)
        top_f = carve(P, 3, TOPK)
        gates = carve(P, 3, TOPK)
        gsum = carve(P, 6)
        onehot = carve(P, 3, TOPK * NE)
        chosen_f = carve(P, 3, NE)
        counts = carve(P, NE)
        n_units = carve(P, NE)
        ends = carve(P, NE)
        zeros_e = carve(P, NE)
        first = carve(P, NE)
        pos = carve(P, 3, NE)
        picked = carve(P, 3, TOPK * NE)
        place = carve(P, 3, TOPK)
        slot_f = carve(P, 3, TOPK)
        unit_f = carve(P, 3, TOPK)
        slot_hot = carve(P, 3 * TOPK, P)
        unit_val = carve(P, 3 * TOPK, 2 * TABW)
        in_unit = carve(P, 3 * TOPK, TABW)
        row_f = carve(P, TABW)
        ended = carve(P, NE)
        expert_col = carve(P, 1)
        x_rows = carve(P, HALF)
        xTu = carve(P, HALF)
        hTu = carve(P, HALF)
        g_min = carve(P, HALF)
        up_clip = carve(P, HALF)
        sig = carve(P, HALF)
        hid = carve(P, HALF)
        y_rows = carve(P, HALF)
        bias_rows = carve(2, 3, HALF)
        place_i = sb("place_i", [P, 3, TOPK], i32)
        slot_i = sb("slot_i", [P, 3, TOPK], i32)
        unit_i = sb("unit_i", [P, 3, TOPK], i32)
        chosen = sb("chosen", [P, 3, NE], bf16)
        final = ring[:, 0, 0:3 * D].rearrange("p (t n) -> p t n", n=D)

        bank = [ctx.enter_context(nc.psum_tensor(f"bank{i}", [P, 512], fp32)) for i in range(8)]
        x1_rows = nc.dram_tensor("x1_rows", [2 * T, HALF], fp32).ap()
        acc_rows = nc.dram_tensor("acc_rows", [2 * T, HALF], fp32).ap()

        def tokens(dram, t):
            first_tok, n = TILES[t]
            return dram[2 * first_tok:2 * (first_tok + n), :].rearrange("(t h) n -> t (h n)", h=2)

        S = {n: sem(n) for n in (
            "x_in params_in gatew_in router_in ln1_in ln2_in acc_written "
            "ident_ok consts_ok pads_ok bd_zero hist_ok "
            "xt_psum xt_dve xt_act chan_psum chan_ok lam_abs lam_exp lam_w lam_ln lam_ok "
            "proj_done xl_ok gl_ok c_ok bank_dve plain_ok xc_ok gates_psum sig_ok gelu_in gelu_t ath_ok one_m mult_ok "
            "x_scaled h_ok sqb_ok rmsb_psum rmsb_in rmsb_ok yb_ok conv_ok gained_ok sqa_ok rmsa_psum rmsa_in rmsa_ok "
            "cv_ok states_ok states_psum states_sb states_dma "
            "lru_psum lru_left out_psum resid_ok var_ok rstd_ok shift_ok norm_ok scaled_ok x1_dma "
            "x1t_psum x1t_dve x1t_act logit_psum gates_zero top_ok exp_ok chosen_ok rank_psum "
            "slot_hot_ok vals_ok tab_psum expert_col_ok expert_psum unit_gate_ok rows_ok tab_ok "
            "rows_zero gath_idx gathered scat_idx bias_in bias_used "
            "gate_done gate_free up_done up_free sig_done glu_ok hid_ok "
            "xu_psum xu_ok hu_psum hu_ok y_done y_ok "
            "ln2_var ln2_rstd ln2_norm out_dma dve_step act_step pool_step").split()}
        slot_loaded = [sem(f"slot_loaded{i}") for i in range(NSLOT)]
        x1_ok, acc_in, ln2_ok = ([sem(f"{n}{t}") for t in range(3)] for n in ("x1_ok", "acc_in", "ln2_ok"))
        half_used = [sem(f"half_used{m}") for m in range(3)]
        product_done = ["gate_done", "up_done", "y_done"]

        block = ctx.enter_context(nc.Block())
        w_in_v = a["w_in"][0].rearrange("(c p) n -> p c n", p=P)
        w_out_v = a["w_out"][0].rearrange("(c p) n -> p c n", p=P)
        experts = [a["exp_w_gate"][0], a["exp_w_up"][0], a["exp_w_down"][0]]
        biases = [a["exp_b_gate"][0], a["exp_b_up"][0], a["exp_b_down"][0]]

        def slot_src(s, e):
            m = experts[s // 2]
            rows = m[e, (s % 2) * HALF:(s % 2 + 1) * HALF, :] if isinstance(e, int) else \
                m[bass.ds(e, 1), (s % 2) * HALF:(s % 2 + 1) * HALF, :].rearrange("o k n -> (o k) n")
            return rows.rearrange("(c p) n -> p c n", p=P)

        def slot(s):
            return ring[:, s, :].rearrange("p (c n) -> p c n", n=D)

        def sample_cols(v_, j):
            w_ = v_[:, j, S0:OW]
            return bass.AP(tensor=w_.tensor, offset=w_.offset, ap=[w_.ap[0], (SEG, NB), (1, DS)])

        def x1_side(act, s_, t):
            n = TILES[t][1]
            act.wait_ge(x1_ok[t], 1)
            s_.mul(scaled[0:n, t, :], x[0:n, t, :], ALPHA).then_inc(S["scaled_ok"], 1)
            if t < 2:
                act.wait_ge(S["x1t_psum"], t + 1)
                s_.copy(xT[:, 4:8, t * P:(t + 1) * P],
                        bank[(3, 5)[t]][:, :].rearrange("p (c n) -> p c n", c=4)).then_inc(S["x1t_act"], 1)

        @block.sync
        def _(sp):
            for t, (t0, n) in enumerate(TILES):
                src = a["x_prompt"][0, t0:t0 + n, :] if t < 2 else a["x_sample"].rearrange("b s d -> (b s) d")
                sp.dma_start(x[0:n, t, :], src).then_inc(S["x_in"], 16)
            for i, (g, s) in enumerate(IN_GROUPS[:3]):
                if i == 1:
                    sp.wait_ge(S["params_in"], 16 * 11)
                sp.dma_start(ring[:, s, :].rearrange("p (c n) -> p c n", n=CW),
                             w_in_v[:, :, g * CW:(g + 1) * CW]).then_inc(slot_loaded[s], 16)
            for s in range(3):
                sp.dma_start(slot(s), slot_src(s, 0)).then_inc(slot_loaded[s], 16)
            for i, (g, s) in enumerate(IN_GROUPS[3:]):
                sp.wait_ge(S["proj_done"], CT * (i + 1))
                sp.dma_start(ring[:, s, :].rearrange("p (c n) -> p c n", n=CW),
                             w_in_v[:, :, g * CW:(g + 1) * CW]).then_inc(slot_loaded[s], 16)
            sp.wait_ge(S["proj_done"], 3 * CT)
            sp.dma_start(slot(5), w_out_v[:, CT:CH, :]).then_inc(slot_loaded[5], 16)
            sp.wait_ge(S["proj_done"], 4 * CT)
            sp.dma_start(slot(3), w_out_v[:, 0:CT, :]).then_inc(slot_loaded[3], 16)
            for s, done, count in ((4, "proj_done", 5 * CT), (5, "lru_psum", 3), (3, "out_psum", 3)):
                sp.wait_ge(S[done], count)
                sp.dma_start(slot(s), slot_src(s, 0)).then_inc(slot_loaded[s], 16)
            for t, (t0, n) in enumerate(TILES):
                sp.wait_ge(x1_ok[t], 1)
                sp.dma_start(tokens(x1_rows, t), x[0:n, t, :]).then_inc(S["x1_dma"], 16)
            for v, name in ((ln_g, "ln2_g"), (ln_b, "ln2_b")):
                sp.dma_start(v[:, :], a[name].partition_broadcast(P).rearrange("p o n -> p (o n)"))\
                    .then_inc(S["ln2_in"], 16)
            sp.wait_ge(S["tab_ok"], 1)
            with sp.Fori(1, NE) as e:
                used = sp.value_load(units_through[0:1, bass.ds(e - 1, 1)], min_val=1, max_val=MAXU)
                for s in range(NSLOT):
                    sp.wait_ge(half_used[s // 2] if s % 2 == 0 else S[product_done[s // 2]], used)
                    sp.dma_start(slot(s), slot_src(s, e)).then_inc(slot_loaded[s], 16)
            n_unit = sp.value_load(units_through[0:1, NE - 1:NE], min_val=NE, max_val=MAXU)
            sp.wait_ge(S["acc_written"], n_unit * 16 + 48)
            for t, (t0, n) in enumerate(TILES):
                sp.dma_start(final[0:n, t, :], tokens(acc_rows, t)).then_inc(acc_in[t], 16)
            for t in (1, 2, 0):
                t0, n = TILES[t]
                sp.wait_ge(ln2_ok[t], 1)
                dst = a["y_prompt"][0, t0:t0 + n, :] if t < 2 else a["y_sample"].rearrange("b s d -> (b s) d")
                sp.dma_start(dst, final[0:n, t, :]).then_inc(S["out_dma"], 16)
            sp.wait_ge(S["out_dma"], 48)
            sp.wait_ge(S["states_dma"], 96)

        @block.gpsimd
        def _(pool):
            g = nc.gpsimd
            step = [0]

            def settle(ins):
                step[0] += 1
                ins.then_inc(S["pool_step"], 1)
                pool.wait_ge(S["pool_step"], step[0])

            settle(g.memset(ident[:, :], 0.0))
            g.affine_select(out=ident[:, :], in_=ident[:, :], compare_op=ALU.not_equal, fill=1.0, base=0,
                            pattern=[[-1, P]], channel_multiplier=1).then_inc(S["ident_ok"], 1)
            g.memset(ones[:, :], 1.0).then_inc(S["consts_ok"], 1)
            settle(g.memset(ones_bf[:, :], 1.0))
            g.affine_select(out=earlier_bf[:, :], in_=ones_bf[:, :], compare_op=ALU.is_gt, fill=0.0, base=0,
                            pattern=[[1, P]], channel_multiplier=-1).then_inc(S["consts_ok"], 1)
            pool.wait_ge(S["consts_ok"], 2)
            settle(g.affine_select(out=half_off[:, :], in_=ones[:, 0:1], compare_op=ALU.is_ge, fill=0.0, base=-UT,
                                   pattern=[[0, 1]], channel_multiplier=1))
            g.tensor_scalar(half_off[:, :], half_off[:, :], -2.0, None, ALU.add).then_inc(S["consts_ok"], 1)
            settle(g.affine_select(out=half_sel[:, :], in_=ones[0:2, :], compare_op=ALU.is_ge, fill=0.0,
                                   base=0, pattern=[[1, P]], channel_multiplier=-UT))
            g.affine_select(out=half_sel[:, :], in_=half_sel[:, :], compare_op=ALU.is_ge, fill=0.0,
                            base=UT - 1, pattern=[[-1, P]], channel_multiplier=UT).then_inc(S["consts_ok"], 1)
            settle(g.iota(iota_i[:, :], pattern=[[1, P]], base=0, channel_multiplier=0))
            g.tensor_copy(iota_e[:, :], iota_i[:, 0:NE]).then_inc(S["consts_ok"], 1)
            g.tensor_copy(iota_s[:, :], iota_i[:, 0:UT]).then_inc(S["consts_ok"], 1)
            settle(g.tensor_copy(iota_u[:, :], iota_i[:, 0:TABW]))
            settle(g.iota(iota_i[:, 0:3], pattern=[[P, 3]], base=1, channel_multiplier=1))
            g.tensor_copy(tok_val[:, :], iota_i[:, 0:3]).then_inc(S["consts_ok"], 1)
            pool.wait_ge(S["chan_ok"], 1)
            samples = slice(S0, FW)

            for j in range(CT):
                last = g.tensor_copy(
                    xl_pad[:, j, samples].rearrange("p (b s) -> p b s", s=SEG)[:, :, 0:3],
                    chan[:, j, ROW_SB:ROW_SB + 3 * NB].rearrange("p (b k) -> p b k", k=3))
                last = g.tensor_copy(
                    cv_pad[:, j, samples].rearrange("p (b s) -> p b s", s=SEG)[:, :, 1:3],
                    chan[:, j, ROW_SA:ROW_SA + 2 * NB].rearrange("p (b k) -> p b k", k=2))
                last.then_inc(S["hist_ok"], 1)
            def put(col, n, src):
                return g.tensor_copy(states[:, :, col:col + n], src)

            def put_samples(j, col, n, src, first_col):
                return g.tensor_copy(
                    states[:, j, col:col + n * NB].rearrange("p (b k) -> p b k", k=n),
                    src.rearrange("p (b s) -> p b s", s=SEG)[:, :, first_col:first_col + n])

            pool.wait_ge(S["xl_ok"], CT)
            put(OUT_PB, 3, xl_pad[:, :, S0 - 3:S0])
            for j in range(CT):
                put_samples(j, OUT_SB, 3, xl_pad[:, j, samples], SEG - 3)
            pool.wait_ge(S["h_ok"], 1)
            put(OUT_PH, 1, xc[:, :, SEQ - 1:SEQ])
            for j in range(CT):
                g.tensor_copy(states[:, j, OUT_SH:OUT_SH + NB], xc[:, j, S0 + DS - 1:OW:SEG])
            pool.wait_ge(S["cv_ok"], 4 * 2)
            put(OUT_PA, 2, cv_pad[:, :, S0 - 2:S0])
            for j in range(CT):
                last = put_samples(j, OUT_SA, 2, cv_pad[:, j, samples], SEG - 2)
            last.then_inc(S["states_ok"], 1)

            pool.wait_ge(S["ln1_in"], 32)
            pool.wait_ge(S["norm_ok"], 1)
            settle(g.tensor_tensor(x[:, 0, :], x[:, 0, :], ln_g[:, :], ALU.mult))
            g.tensor_tensor(x[:, 0, :], x[:, 0, :], ln_b[:, :], ALU.add).then_inc(x1_ok[0], 1)
            for t, (t0, n) in enumerate(TILES):
                pool.wait_ge(S["scaled_ok"], t + 1)
                pool.dma_start(tokens(acc_rows, t), scaled[0:n, t, :]).then_inc(S["acc_written"], 16)

            g.memset(x_rows, 0.0).then_inc(S["rows_zero"], 1)
            bound = pool.to_reg(2 * T - 1)

            def gather(rows):
                g.indirect_dma_start(out=x_rows, out_offset=None, in_=x1_rows[:, :],
                                     in_offset=bass.IndirectOffsetOnAxis(ap=rows.bitcast(u32), axis=0),
                                     bounds_check=bound, oob_is_err=False).then_inc(S["gathered"], 16)

            def bias_load(e):
                for m in range(3):
                    src = biases[m][e, :].rearrange("(h n) -> h n", h=2) if isinstance(e, int) else \
                        biases[m][bass.ds(e, 1), :].rearrange("o (h n) -> (o h) n", h=2)
                    pool.dma_start(bias_rows[:, m, :], src).then_inc(S["bias_in"], 16)

            pool.wait_ge(S["states_dma"], 96)
            bias_load(0)
            pool.wait_ge(S["x1_dma"], 48)
            pool.wait_ge(S["rows_zero"], 1)
            pool.wait_ge(S["rows_ok"], 1)
            gather(unit_rows[:, 0:1])
            pool.wait_ge(S["tab_ok"], 1)
            n_unit = pool.value_load(units_through[0:1, NE - 1:NE], min_val=NE, max_val=MAXU)
            with pool.Fori(0, n_unit) as u:
                u2 = pool.to_reg(u + 2)
                pool.wait_ge(S["gathered"], u * 16 + 16)
                g.tensor_copy(rows_g[:, :], unit_rows[:, bass.ds(u + 1, 1)]).then_inc(S["gath_idx"], 1)
                pool.wait_ge(S["x1_dma"], 48)
                pool.wait_ge(S["gath_idx"], u + 1)
                pool.wait_ge(S["xu_psum"], u + 1)
                gather(rows_g[:, 0:1])
                e = pool.value_load(unit_expert[0:1, bass.ds(u + 1, 1)], min_val=0, max_val=NE - 1)
                pool.wait_ge(S["bias_used"], u + 1)
                bias_load(e)
                pool.wait_ge(S["acc_written"], u * 16 + 48)
                g.tensor_copy(rows_s[:, :], unit_rows[:, bass.ds(u, 1)]).then_inc(S["scat_idx"], 1)
                pool.wait_ge(S["x1_dma"], 48)
                pool.wait_ge(S["scat_idx"], u + 1)
                pool.wait_ge(S["y_ok"], u2)
                g.indirect_dma_start(out=acc_rows[:, :],
                                     out_offset=bass.IndirectOffsetOnAxis(ap=rows_s[:, 0:1].bitcast(u32), axis=0),
                                     in_=y_rows, in_offset=None, bounds_check=bound, oob_is_err=False,
                                     compute_op=ALU.add).then_inc(S["acc_written"], 16)
            pool.wait_ge(S["gathered"], n_unit * 16 + 16)
            pool.wait_ge(S["bias_in"], n_unit * 48 + 48)
            pool.wait_ge(S["acc_written"], n_unit * 16 + 48)
            pool.wait_ge(S["ln2_in"], 32)
            pool.wait_ge(S["ln2_norm"], 1)
            settle(g.tensor_tensor(final[:, 0, :], final[:, 0, :], ln_g[:, :], ALU.mult))
            g.tensor_tensor(final[:, 0, :], final[:, 0, :], ln_b[:, :], ALU.add).then_inc(ln2_ok[0], 1)

        @block.scalar
        def _(act):
            s_ = nc.scalar
            step = [0]

            def settle(ins):
                step[0] += 1
                ins.then_inc(S["act_step"], 1)
                act.wait_ge(S["act_step"], step[0])

            for row, name, n in ((ROW_WA, "conv_a_w", 3), (ROW_WB, "conv_b_w", 4)):
                act.dma_start(params[row:row + n, :], a[name][0]).then_inc(S["params_in"], 16)
            for row, name in ((ROW_CB, "conv_b_b"), (ROW_BA, "lru_ba"), (ROW_BI, "lru_bi"), (ROW_LAM, "lru_lambda"),
                              (ROW_GA, "gn_a"), (ROW_GB, "gn_b")):
                act.dma_start(params[row:row + 1, :], a[name]).then_inc(S["params_in"], 16)
            act.dma_start(params[ROW_SA:ROW_SB, :], a["state_conv_a"][0].rearrange("b k c -> (b k) c"))\
                .then_inc(S["params_in"], 16)
            act.dma_start(params[ROW_SB:ROW_H0, :], a["state_conv_b"][0].rearrange("b k c -> (b k) c"))\
                .then_inc(S["params_in"], 16)
            act.dma_start(params[ROW_H0:ROWS, :], a["state_lru_h"][0]).then_inc(S["params_in"], 16)
            act.wait_ge(S["bd_zero"], 1)
            for dst, name in ((wa_bd, "lru_wa"), (wi_bd, "lru_wi")):
                for odd in range(2):
                    act.dma_start(dst[64 * odd:64 * odd + 64, :, 64 * odd:64 * odd + 64],
                                  a[name][0].rearrange("(j two) i o -> two i j o", two=2)[odd])\
                        .then_inc(S["gatew_in"], 16)
            act.dma_start(router_w[:, :, :], a["router_w"][0].rearrange("(c p) e -> p c e", p=P))\
                .then_inc(S["router_in"], 16)
            act.dma_start(router_b[:, :], a["router_b"].partition_broadcast(P).rearrange("p o n -> p (o n)"))\
                .then_inc(S["router_in"], 16)
            for v, name in ((ln_g, "ln1_g"), (ln_b, "ln1_b")):
                act.dma_start(v[:, :], a[name].partition_broadcast(P).rearrange("p o n -> p (o n)"))\
                    .then_inc(S["ln1_in"], 16)
            act.wait_ge(S["lam_abs"], 1)
            s_.activation(small[:, 1, :], small[:, 0, :], ACT.Exp, scale=-1.0).then_inc(S["lam_exp"], 1)
            act.wait_ge(S["lam_w"], 1)
            s_.activation(small[:, 3, :], small[:, 2, :], ACT.Ln).then_inc(S["lam_ln"], 1)
            for j in range(CT):
                act.wait_ge(S["proj_done"], j + 1)
                s_.copy(xl_pad[:, j, HIST:S0], bank[j][:, 0:SEQ])
                s_.copy(xl_pad[:, j, S0:FW].rearrange("p (b s) -> p b s", s=SEG)[:, :, HIST:SEG],
                        bank[j][:, SEQ:T].rearrange("p (b s) -> p b s", s=DS)).then_inc(S["xl_ok"], 1)
            for j in range(CT):
                act.wait_ge(S["proj_done"], CT + j + 1)
                s_.copy(gl[:, j, :], bank[j][:, 0:T]).then_inc(S["gl_ok"], 1)
            def gate_sigmoids(j):
                act.wait_ge(S["gates_psum"], j + 1)
                s_.activation(decay[:, j, :], bank[4][:, 0:OW], ACT.Sigmoid, bias=chan[:, j, ROW_BA:ROW_BA + 1])
                s_.activation(drive[:, j, :], bank[5][:, 0:OW], ACT.Sigmoid, bias=chan[:, j, ROW_BI:ROW_BI + 1])\
                    .then_inc(S["sig_ok"], 1)

            for j in range(CT):
                act.wait_ge(S["proj_done"], 2 * CT + j + 1)
                s_.copy(gate_c[:, j, :], bank[j][:, 0:T]).then_inc(S["c_ok"], 1)
                gate_sigmoids(j)
            act.wait_ge(S["gelu_in"], 1)
            s_.activation(tmp[:, :, 0:T], tmp[:, :, 0:T], ACT.Tanh, scale=GELU_B).then_inc(S["gelu_t"], 1)
            act.wait_ge(S["lam_ok"], 1)
            act.wait_ge(S["sig_ok"], CT)
            for j in range(CT):
                settle(s_.activation(mult[:, j, :], decay[:, j, :], ACT.Tanh, scale=lam8[:, 1, j:j + 1]))
                s_.activation(decay[:, j, :], decay[:, j, :], ACT.Exp, scale=lam8[:, 0, j:j + 1])\
                    .then_inc(S["ath_ok"], 1)
            act.wait_ge(S["one_m"], 1)
            s_.activation(mult, mult, ACT.Sqrt).then_inc(S["mult_ok"], 1)
            act.wait_ge(S["xt_psum"], 3)
            for t, (t0, n) in enumerate(TILES):
                last = s_.mul(x[0:n, t, :], x[0:n, t, :], ALPHA)
            last.then_inc(S["x_scaled"], 1)
            act.wait_ge(S["sqb_ok"], 1)
            for j in range(CT):
                last = s_.mul(mixT[:, CT + j, :], mixT[:, CT + j, :], chan[:, j, ROW_GB:ROW_GB + 1])
            last.then_inc(S["yb_ok"], 1)
            for j in range(CT):
                act.wait_ge(S["conv_ok"], j + 1)
                s_.mul(conv_gained[:, j, :], conv_a[:, j, :], chan[:, j, ROW_GA:ROW_GA + 1])\
                    .then_inc(S["gained_ok"], 1)
            act.wait_ge(S["rmsb_in"], 1)
            s_.activation(rms[:, 0:2], rms[:, 0:2], ACT.Sqrt)
            s_.activation(rms[0:UT, 2:3], rms[0:UT, 2:3], ACT.Sqrt).then_inc(S["rmsb_ok"], 1)
            act.wait_ge(S["plain_ok"], CT)
            s_.activation(tmp[:, :, 0:T], plain_a[:, :, 0:T], ACT.Square).then_inc(S["sqa_ok"], 1)
            act.wait_ge(S["rmsa_in"], 1)
            s_.activation(rms[:, 3:5], rms[:, 3:5], ACT.Sqrt)
            s_.activation(rms[0:UT, 5:6], rms[0:UT, 5:6], ACT.Sqrt).then_inc(S["rmsa_ok"], 1)
            act.wait_ge(S["states_psum"], 1)
            s_.copy(states_out, bank[6][0:OUTS, :]).then_inc(S["states_sb"], 1)
            act.wait_ge(S["states_sb"], 1)
            for name, col, n in (("prompt_conv_a", OUT_PA, 2), ("prompt_conv_b", OUT_PB, 3), ("prompt_lru_h", OUT_PH, 1),
                                 ("sample_conv_a", OUT_SA, 16), ("sample_conv_b", OUT_SB, 24),
                                 ("sample_lru_h", OUT_SH, 8)):
                dst = a[name][0]
                if "conv" in name:
                    dst = dst.rearrange("b k c -> (b k) c")
                act.dma_start(dst, states_out[col:col + n, :]).then_inc(S["states_dma"], 16)
            for t, (t0, n) in enumerate(TILES):
                act.wait_ge(S["var_ok"], t + 1)
                s_.activation(rstd[0:n, t:t + 1], rstd[0:n, t:t + 1], ACT.Sqrt).then_inc(S["rstd_ok"], 1)
                act.wait_ge(S["shift_ok"], t + 1)
                s_.activation(x[0:n, t, :], x[0:n, t, :], ACT.Identity, bias=shift[0:n, t:t + 1],
                              scale=rstd[0:n, t:t + 1]).then_inc(S["norm_ok"], 1)
                if t:
                    x1_side(act, s_, t - 1)
            x1_side(act, s_, 2)
            for t, (t0, n) in enumerate(TILES):
                act.wait_ge(S["top_ok"], t + 1)
                s_.activation(gates[0:n, t, :], top_v[0:n, t, 0:TOPK], ACT.Exp, bias=gsum[0:n, t:t + 1],
                              accum_out=gsum[0:n, 3 + t:4 + t]).then_inc(S["exp_ok"], 1)
            act.wait_ge(S["slot_hot_ok"], 1)
            s_.copy(slot_hot[:, :, UT:P], slot_hot[:, :, 0:UT]).then_inc(S["slot_hot_ok"], 1)
            act.wait_ge(S["xu_psum"], 1)
            s_.copy(xTu, bank[3][:, :]).then_inc(S["xu_ok"], 1)

            act.wait_ge(S["tab_ok"], 1)
            n_unit = act.value_load(units_through[0:1, NE - 1:NE], min_val=NE, max_val=MAXU)
            with act.Fori(0, n_unit) as u:
                act.wait_ge(S["gate_free"], u + 2)
                s_.activation(sig, g_min, ACT.Sigmoid, scale=SWISH).then_inc(S["sig_done"], 1)
                act.wait_ge(S["xu_psum"], u + 2)
                s_.copy(xTu, bank[3][:, :]).then_inc(S["xu_ok"], 1)
                act.wait_ge(S["hu_psum"], u + 1)
                s_.copy(hTu, bank[4][:, :]).then_inc(S["hu_ok"], 1)
                act.wait_ge(S["y_done"], u + 1)
                act.wait_ge(S["acc_written"], u * 16 + 48)
                s_.activation(y_rows, bank[2][:, :], ACT.Copy, scale=unit_gate[:, bass.ds(u, 1)])\
                    .then_inc(S["y_ok"], 1)

            for t, (t0, n) in enumerate(TILES):
                act.wait_ge(S["ln2_var"], 2 * t + 1)
                s_.activation(rstd[0:n, t:t + 1], rstd[0:n, t:t + 1], ACT.Sqrt).then_inc(S["ln2_rstd"], 1)
                act.wait_ge(S["ln2_var"], 2 * t + 2)
                s_.activation(final[0:n, t, :], final[0:n, t, :], ACT.Identity, bias=shift[0:n, t:t + 1],
                              scale=rstd[0:n, t:t + 1]).then_inc(S["ln2_norm"], 1)

        @block.vector
        def _(dve):
            v = nc.vector
            step = [0]

            def settle(ins):
                step[0] += 1
                ins.then_inc(S["dve_step"], 1)
                dve.wait_ge(S["dve_step"], step[0])

            v.memset(wa_bd, 0.0)
            v.memset(wi_bd, 0.0).then_inc(S["bd_zero"], 1)
            v.memset(xl_pad[:, :, 0:HIST], 0.0)
            v.memset(cv_pad[:, :, 0:HIST], 0.0)
            v.memset(cv_pad[:, :, S0:FW].rearrange("p c (b s) -> p c b s", s=SEG)[:, :, :, 0], 0.0)\
                .then_inc(S["pads_ok"], 1)
            for t in range(3):
                dve.wait_ge(S["xt_psum"], t + 1)
                if t < 2:
                    for h_ in range(2):
                        last = v.tensor_copy(xT[:, 4 * h_:4 * h_ + 4, t * P:(t + 1) * P],
                                             bank[2 * t + h_][:, :].rearrange("p (c n) -> p c n", c=4))
                else:
                    last = v.tensor_copy(xT[:, :, 2 * P:T], bank[4][:, :].rearrange("p (c n) -> p c n", c=CH))
                last.then_inc(S["xt_dve"], 1)
            dve.wait_ge(S["chan_psum"], 1)
            v.tensor_copy(chan[:, :, 0:ROWS], bank[6][:, 0:CT * 64].rearrange("p (c n) -> p c n", c=CT)[:, :, 0:ROWS])\
                .then_inc(S["chan_ok"], 1)
            dve.wait_ge(S["chan_ok"], 1)
            lam = chan[:, :, ROW_LAM]
            ab, q, w, lnw, d, rec, res, extra = (small[:, i, :] for i in range(8))
            v.scalar_tensor_tensor(ab, lam, -1.0, lam, ALU.mult, ALU.max).then_inc(S["lam_abs"], 1)
            dve.wait_ge(S["lam_exp"], 1)
            v.tensor_scalar(w, q, 1.0, None, ALU.add).then_inc(S["lam_w"], 1)
            dve.wait_ge(S["lam_w"], 1)
            settle(v.tensor_scalar(d, w, -1.0, None, ALU.add))
            settle(v.tensor_scalar(rec, d, 1e-30, None, ALU.max))
            settle(v.reciprocal(rec, rec))
            settle(v.tensor_tensor(rec, rec, q, ALU.mult))
            settle(v.tensor_scalar(extra, d, 0.0, None, ALU.is_equal))
            settle(v.tensor_tensor(extra, extra, q, ALU.mult))
            dve.wait_ge(S["lam_ln"], 1)
            settle(v.tensor_tensor(res, lnw, rec, ALU.mult))
            settle(v.tensor_tensor(res, res, extra, ALU.add))
            settle(v.tensor_scalar(extra, lam, -1.0, 0.0, ALU.mult, ALU.max))
            settle(v.tensor_tensor(res, res, extra, ALU.add))
            v.tensor_scalar(lam8[:, 0, :], res, -LRU_C, None, ALU.mult)
            v.tensor_scalar(lam8[:, 1, :], res, LRU_C, None, ALU.mult).then_inc(S["lam_ok"], 1)

            dve.wait_ge(S["hist_ok"], CT)
            dve.wait_ge(S["pads_ok"], 1)
            for j in range(CT):
                dve.wait_ge(S["xl_ok"], j + 1)
                settle(v.tensor_scalar(xc[:, j, :], xl_pad[:, j, 0:OW], chan[:, j, ROW_WB:ROW_WB + 1],
                                       chan[:, j, ROW_CB:ROW_CB + 1], ALU.mult, ALU.add))
                for k in range(1, 4):
                    last = v.scalar_tensor_tensor(xc[:, j, :], xl_pad[:, j, k:k + OW],
                                                  chan[:, j, ROW_WB + k:ROW_WB + k + 1], xc[:, j, :],
                                                  ALU.mult, ALU.add)
                    if k < 3:
                        settle(last)
                last.then_inc(S["xc_ok"], 1)
            arg = tmp[:, :, 0:T]
            dve.wait_ge(S["gl_ok"], CT)
            settle(v.tensor_tensor(arg, gl, gl, ALU.mult))
            settle(v.tensor_scalar(arg, arg, GELU_A, 1.0, ALU.mult, ALU.add))
            v.tensor_tensor(arg, arg, gl, ALU.mult).then_inc(S["gelu_in"], 1)
            dve.wait_ge(S["gelu_t"], 1)
            settle(v.scalar_tensor_tensor(gl, arg, 1.0, gl, ALU.add, ALU.mult))

            def masked_v(j):
                dve.wait_ge(S["proj_done"], 3 * CT + j + 1)
                v.tensor_tensor(cv_pad[:, j, HIST:S0], bank[j][:, 0:SEQ], gate_c[:, j, 0:SEQ], ALU.mult)\
                    .then_inc(S["cv_ok"], 1)
                v.tensor_tensor(cv_pad[:, j, S0:FW].rearrange("p (b s) -> p b s", s=SEG)[:, :, HIST:SEG],
                                bank[j][:, SEQ:T].rearrange("p (b s) -> p b s", s=DS),
                                gate_c[:, j, SEQ:T].rearrange("p (b s) -> p b s", s=DS), ALU.mult)\
                    .then_inc(S["cv_ok"], 1)

            dve.wait_ge(S["ath_ok"], CT)
            settle(v.tensor_tensor(tmp, decay, decay, ALU.mult))
            v.scalar_tensor_tensor(mult, tmp, 1.0, mult, ALU.add, ALU.mult).then_inc(S["one_m"], 1)
            settle(v.tensor_tensor(drive, drive, xc, ALU.mult))
            dve.wait_ge(S["c_ok"], CT)
            masked_v(0)
            dve.wait_ge(S["mult_ok"], 1)
            settle(v.tensor_tensor(drive, drive, mult, ALU.mult))
            for j in range(CT):
                v.memset(decay[:, j, 0:1], 0.0)
                v.memset(decay[:, j, S0 - 1:OW:SEG], 0.0)
                last = v.tensor_copy(drive[:, j, S0 - 1:OW:SEG], chan[:, j, ROW_H0:ROW_H0 + NB])
            settle(last)
            h = xc.rearrange("p c w -> p (c w)")
            v.tensor_tensor_scan(h, decay.rearrange("p c w -> p (c w)"), drive.rearrange("p c w -> p (c w)"),
                                 0.0, ALU.mult, ALU.add).then_inc(S["h_ok"], 1)
            masked_v(1)
            dve.wait_ge(S["h_ok"], 1)
            settle(v.scalar_tensor_tensor(mixT[:, CT:CH, 0:SEQ], gl[:, :, 0:SEQ], 0.5, xc[:, :, 0:SEQ],
                                          ALU.mult, ALU.mult))
            for j in range(CT):
                last = v.scalar_tensor_tensor(
                    mixT[:, CT + j, SEQ:T].rearrange("p (b s) -> p b s", s=DS),
                    gl[:, j, SEQ:T].rearrange("p (b s) -> p b s", s=DS), 0.5,
                    sample_cols(xc, j), ALU.mult, ALU.mult)
            settle(last)
            sq = tmp[:, :, 0:T]
            v.tensor_tensor(sq, mixT[:, CT:CH, :], mixT[:, CT:CH, :], ALU.mult).then_inc(S["sqb_ok"], 1)

            def conv_a_tile(j):
                dve.wait_ge(S["cv_ok"], 2 * (j + 1))
                settle(v.tensor_scalar(conv_a[:, j, :], cv_pad[:, j, 1:1 + OW], chan[:, j, ROW_WA:ROW_WA + 1],
                                       None, ALU.mult))
                for k in range(1, 3):
                    last = v.scalar_tensor_tensor(conv_a[:, j, :], cv_pad[:, j, 1 + k:1 + k + OW],
                                                  chan[:, j, ROW_WA + k:ROW_WA + k + 1], conv_a[:, j, :],
                                                  ALU.mult, ALU.add)
                    if k == 1:
                        settle(last)
                last.then_inc(S["conv_ok"], 1)

            def gated_a(j):
                dve.wait_ge(S["proj_done"], 4 * CT + j + 1)
                dve.wait_ge(S["gained_ok"], j + 1)
                for dst, conv, s in ((mixT[:, j, :], conv_gained, "bank_dve"), (plain_a[:, j, 0:T], conv_a, "plain_ok")):
                    v.tensor_tensor(dst[:, 0:SEQ], bank[j][:, 0:SEQ], conv[:, j, 0:SEQ], ALU.mult)
                    v.tensor_tensor(dst[:, SEQ:T].rearrange("p (b s) -> p b s", s=DS),
                                    bank[j][:, SEQ:T].rearrange("p (b s) -> p b s", s=DS), sample_cols(conv, j),
                                    ALU.mult).then_inc(S[s], 1)

            masked_v(2)
            masked_v(3)
            for j in range(CT):
                conv_a_tile(j)

            def inv_rms_in(col, s):
                for n, c0, c1 in ((P, col, col + 2), (UT, col + 2, col + 3)):
                    last = v.tensor_scalar(rms[0:n, c0:c1], bank[7][0:n, c0:c1], 1.0 / CW, RMS_EPS, ALU.mult, ALU.add)
                settle(last)
                v.reciprocal(rms[:, col:col + 2], rms[:, col:col + 2])
                v.reciprocal(rms[0:UT, col + 2:col + 3], rms[0:UT, col + 2:col + 3]).then_inc(S[s], 1)

            gated_a(0)
            gated_a(1)
            dve.wait_ge(S["rmsb_psum"], 1)
            inv_rms_in(0, "rmsb_in")
            gated_a(2)
            gated_a(3)

            def add_product(t, banks, col, s):
                n = TILES[t][1]
                for h_ in range(2):
                    src = banks[h_][0:n, :] if t < 2 else banks[h_][UT * h_:UT * h_ + UT, :]
                    last = v.scalar_tensor_tensor(x[0:n, t, h_ * 512:(h_ + 1) * 512], src, rms[0:n, col + t:col + t + 1],
                                                  x[0:n, t, h_ * 512:(h_ + 1) * 512], ALU.mult, ALU.add)
                last.then_inc(S[s], 1)

            dve.wait_ge(S["rmsb_ok"], 1)
            dve.wait_ge(S["x_scaled"], 1)
            for t in range(3):
                dve.wait_ge(S["lru_psum"], t + 1)
                add_product(t, [bank[i] for i in LRU_BANKS[t]], 0, "lru_left")
                if t == 0:
                    dve.wait_ge(S["rmsa_psum"], 1)
                    inv_rms_in(3, "rmsa_in")
            dve.wait_ge(S["rmsa_ok"], 1)

            def moments(src, t, n, s):
                v.bn_stats(stats[0:n, t, 0:6], src[0:n, t, 0:512])
                settle(v.bn_stats(stats[0:n, t, 6:12], src[0:n, t, 512:1024]))
                settle(v.bn_aggr(mean_var[0:n, t, :], stats[0:n, t, :].rearrange("p (a b) -> p a b", b=6)))
                settle(v.tensor_scalar(rstd[0:n, t:t + 1], mean_var[0:n, t, 1:2], LN_EPS, None, ALU.add))
                v.reciprocal(rstd[0:n, t:t + 1], rstd[0:n, t:t + 1]).then_inc(S[s], 1)

            def offset(t, n, s):
                v.scalar_tensor_tensor(shift[0:n, t:t + 1], mean_var[0:n, t, 0:1], -1.0, rstd[0:n, t:t + 1],
                                       ALU.mult, ALU.mult).then_inc(S[s], 1)

            def affine(dst, t, n, s):
                settle(v.tensor_tensor(dst[0:n, t, :], dst[0:n, t, :], ln_g[0:n, :], ALU.mult))
                v.tensor_tensor(dst[0:n, t, :], dst[0:n, t, :], ln_b[0:n, :], ALU.add).then_inc(s, 1)

            dve.wait_ge(S["ln1_in"], 32)

            def residual(t):
                n = TILES[t][1]
                dve.wait_ge(S["out_psum"], t + 1)
                dve.wait_ge(S["lru_left"], t + 1)
                add_product(t, [bank[i] for i in CONV_BANKS[t]], 3, "resid_ok")
                dve.wait_ge(S["resid_ok"], t + 1)
                moments(x, t, n, "var_ok")
                dve.wait_ge(S["rstd_ok"], t + 1)
                offset(t, n, "shift_ok")

            def finish_norm(t):
                n = TILES[t][1]
                dve.wait_ge(S["norm_ok"], t + 1)
                affine(x, t, n, x1_ok[t])

            def x1t(t):
                dve.wait_ge(S["x1t_psum"], t + 1)
                if t < 2:
                    v.tensor_copy(xT[:, 0:4, t * P:(t + 1) * P],
                                  bank[(2, 4)[t]][:, :].rearrange("p (c n) -> p c n", c=4)).then_inc(S["x1t_dve"], 1)
                else:
                    v.tensor_copy(xT[:, :, 2 * P:T], bank[0][:, :].rearrange("p (c n) -> p c n", c=CH))\
                        .then_inc(S["x1t_dve"], 1)

            def best_experts(t):
                n = TILES[t][1]
                dve.wait_ge(S["logit_psum"], t + 1)
                settle(v.tensor_tensor(logits[0:n, t, :], bank[LOGIT_BANKS[t]][0:n, 0:NE], router_b[0:n, :], ALU.add))
                settle(v.max(top_v[0:n, t, :], logits[0:n, t, :]))
                v.tensor_scalar(gsum[0:n, t:t + 1], top_v[0:n, t, 0:1], -1.0, None, ALU.mult).then_inc(S["top_ok"], 1)
                settle(v.max_index(top_i[0:n, t, :].bitcast(u32), top_v[0:n, t, :], logits[0:n, t, :]))
                settle(v.tensor_copy(top_f[0:n, t, :], top_i[0:n, t, 0:TOPK].bitcast(u32)))
                hot = onehot[0:n, t, :].rearrange("p (k e) -> p k e", e=NE)
                settle(v.tensor_tensor(hot, iota_e[0:n, :].unsqueeze(1).to_broadcast([n, TOPK, NE]),
                                       top_f[0:n, t, :].unsqueeze(2).to_broadcast([n, TOPK, NE]), ALU.is_equal))
                settle(v.reduce_sum(chosen_f[0:n, t, :], hot.rearrange("p k e -> p e k"), AX.X))
                v.tensor_copy(chosen[0:n, t, :], chosen_f[0:n, t, :]).then_inc(S["chosen_ok"], 1)

            def normed_gates(t):
                n = TILES[t][1]
                dve.wait_ge(S["exp_ok"], t + 1)
                settle(v.reciprocal(gsum[0:n, 3 + t:4 + t], gsum[0:n, 3 + t:4 + t]))
                settle(v.tensor_scalar(gates[0:n, t, :], gates[0:n, t, :], gsum[0:n, 3 + t:4 + t], None, ALU.mult))

            residual(0)
            residual(1)
            v.memset(zeros_e, 0.0)
            v.memset(gates[UT:P, 2, :], 0.0)
            settle(v.memset(onehot[UT:P, 2, :], 0.0))
            finish_norm(1)
            residual(2)
            x1t(0)
            finish_norm(2)
            x1t(1)
            dve.wait_ge(S["router_in"], 32)
            best_experts(0)
            x1t(2)
            best_experts(1)
            normed_gates(0)
            best_experts(2)
            normed_gates(1)
            dve.wait_ge(S["rank_psum"], 1)
            counts = bank[6][:, 3 * NE:4 * NE]
            settle(v.tensor_scalar(n_units, counts, float(UT), 1.0, ALU.is_gt, ALU.add))
            for k in range(2, T // UT):
                settle(v.scalar_tensor_tensor(n_units, counts, float(k * UT), n_units, ALU.is_gt, ALU.add))
            settle(v.tensor_tensor_scan(ends, n_units, zeros_e, 0.0, ALU.add, ALU.add))
            settle(v.tensor_tensor(first, ends, n_units, ALU.subtract))
            settle(v.scalar_tensor_tensor(pos, first.unsqueeze(1).to_broadcast([P, 3, NE]), float(UT),
                                          bank[6][:, 0:3 * NE].rearrange("p (t e) -> p t e", e=NE),
                                          ALU.mult, ALU.add))
            picks = picked.rearrange("p t (k e) -> p t k e", e=NE)
            settle(v.tensor_tensor(picks, onehot.rearrange("p t (k e) -> p t k e", e=NE),
                                   pos.unsqueeze(2).to_broadcast([P, 3, TOPK, NE]), ALU.mult))
            settle(v.reduce_sum(place, picks, AX.X))
            settle(v.tensor_copy(place_i[:, :, :], place))
            v.tensor_scalar(slot_i[:, :, :], place_i[:, :, :], UT - 1, None, ALU.bitwise_and)
            settle(v.tensor_scalar(unit_i[:, :, :], place_i[:, :, :], UT.bit_length() - 1, None,
                                   ALU.logical_shift_right))
            v.tensor_copy(slot_f, slot_i[:, :, :])
            settle(v.tensor_copy(unit_f, unit_i[:, :, :]))
            v.tensor_tensor(slot_hot[:, :, 0:UT], iota_s[:, :].unsqueeze(1).to_broadcast([P, 3 * TOPK, UT]),
                            slot_f.rearrange("p t k -> p (t k)").unsqueeze(2).to_broadcast([P, 3 * TOPK, UT]),
                            ALU.is_equal).then_inc(S["slot_hot_ok"], 1)
            settle(v.tensor_tensor(in_unit, iota_u[:, :].unsqueeze(1).to_broadcast([P, 3 * TOPK, TABW]),
                                   unit_f.rearrange("p t k -> p (t k)").unsqueeze(2)
                                   .to_broadcast([P, 3 * TOPK, TABW]), ALU.is_equal))
            v.tensor_tensor(unit_val[:, :, 0:TABW].rearrange("p (t k) u -> p t k u", k=TOPK),
                            in_unit.rearrange("p (t k) u -> p t k u", k=TOPK),
                            tok_val[:, :].unsqueeze(2).unsqueeze(3).to_broadcast([P, 3, TOPK, TABW]), ALU.mult)
            normed_gates(2)
            v.tensor_tensor(unit_val[:, :, TABW:2 * TABW], in_unit,
                            gates.rearrange("p t k -> p (t k)").unsqueeze(2).to_broadcast([P, 3 * TOPK, TABW]),
                            ALU.mult).then_inc(S["vals_ok"], 1)
            v.tensor_copy(units_through[:, :], ends[0:1, :])
            settle(v.tensor_scalar(ended, ends, tok_val[:, 0:1], None, ALU.is_lt))
            v.reduce_sum(expert_col, ended, AX.X).then_inc(S["expert_col_ok"], 1)
            dve.wait_ge(S["tab_psum"], 1)
            settle(v.tensor_scalar(row_f, bank[7][:, 0:TABW], 0.0, EMPTY, ALU.is_equal, ALU.mult))
            settle(v.scalar_tensor_tensor(row_f, bank[7][:, 0:TABW], 2.0, row_f, ALU.mult, ALU.add))
            v.tensor_scalar(unit_rows[:, :], row_f, half_off[:, 0:1], None, ALU.add).then_inc(S["rows_ok"], 1)
            dve.wait_ge(S["expert_psum"], 1)
            v.tensor_copy(unit_gate[:, :], bank[7][:, TABW:2 * TABW]).then_inc(S["unit_gate_ok"], 1)
            dve.wait_ge(S["unit_gate_ok"], 1)
            v.tensor_scalar(unit_expert[:, :], bank[2][0:1, 0:TABW], float(NE - 1), None, ALU.min)\
                .then_inc(S["tab_ok"], 1)

            dve.wait_ge(S["tab_ok"], 1)
            dve.sem_inc(S["gate_free"], 1)
            dve.sem_inc(S["up_free"], 1)
            dve.sem_inc(S["y_ok"], 1)
            n_unit = dve.value_load(units_through[0:1, NE - 1:NE], min_val=NE, max_val=MAXU)
            with dve.Fori(0, n_unit) as u:
                dve.wait_ge(S["gate_done"], u + 1)
                v.tensor_scalar(g_min, bank[0][:, :], LIMIT, None, ALU.min).then_inc(S["gate_free"], 1)
                dve.wait_ge(S["sig_done"], u + 1)
                v.tensor_tensor(g_min, g_min, sig, ALU.mult).then_inc(S["glu_ok"], 1)
                dve.wait_ge(S["up_done"], u + 1)
                v.tensor_scalar(up_clip, bank[1][:, :], LIMIT, -LIMIT, ALU.min, ALU.max).then_inc(S["up_free"], 1)
                dve.wait_ge(S["up_free"], u + 2)
                dve.wait_ge(S["glu_ok"], u + 1)
                v.scalar_tensor_tensor(hid, up_clip, 1.0, g_min, ALU.add, ALU.mult).then_inc(S["hid_ok"], 1)

            dve.wait_ge(S["ln2_in"], 32)

            for t, (t0, n) in enumerate(TILES):
                dve.wait_ge(acc_in[t], 16)
                moments(final, t, n, "ln2_var")
                dve.wait_ge(S["ln2_rstd"], t + 1)
                offset(t, n, "ln2_var")
            for t in (1, 2):
                dve.wait_ge(S["ln2_norm"], t + 1)
                affine(final, t, TILES[t][1], ln2_ok[t])

        @block.tensor
        def _(pe):
            mm = nc.tensor.matmul
            pe.wait_ge(S["ident_ok"], 1)
            pe.wait_ge(S["x_in"], 48)
            for t, (t0, n) in enumerate(TILES):
                for c in range(CH):
                    b, col = (2 * t + c // 4, (c % 4) * P) if t < 2 else (4, c * n)
                    last = nc.tensor.transpose(bank[b][:, col:col + n], x[0:n, t, c * P:(c + 1) * P],
                                               ident[0:n, 0:n])
                last.then_inc(S["xt_psum"], 1)
            pe.wait_ge(S["xt_dve"], 3)

            def by_channel():
                pe.wait_ge(S["params_in"], 16 * 11)
                for j in range(CT):
                    last = nc.tensor.transpose(bank[6][:, j * 64:j * 64 + ROWS], params[:, j * P:(j + 1) * P],
                                               ident[0:ROWS, 0:ROWS])
                last.then_inc(S["chan_psum"], 1)

            def gate_products(j):
                pe.wait_ge(S["xc_ok"], j + 1)
                if j:
                    pe.wait_ge(S["sig_ok"], j)
                mm(bank[4][:, 0:OW], wa_bd[:, j, :], xc[:, j, :], start=True, stop=True)
                mm(bank[5][:, 0:OW], wi_bd[:, j, :], xc[:, j, :], start=True, stop=True)\
                    .then_inc(S["gates_psum"], 1)

            def sum_squares(col, ok, s):
                pe.wait_ge(S[ok], 1)
                for t, (t0, n) in enumerate(TILES):
                    for j in range(CT):
                        last = mm(bank[7][0:n, col + t:col + t + 1], tmp[:, j, t0:t0 + n], ones[:, 0:1],
                                  start=j == 0, stop=j == CT - 1)
                last.then_inc(S[s], 1)

            freed = {1: ("xl_ok", 1), 2: ("gl_ok", 1), 3: ("c_ok", 1), 4: ("cv_ok", 2)}
            seen = [0] * NSLOT
            for gi, (g, s) in enumerate(IN_GROUPS):
                seen[s] += 1
                pe.wait_ge(slot_loaded[s], 16 * seen[s])
                w = ring[:, s, :].rearrange("p (c n) -> p c n", n=CW)
                for j in range(CT):
                    if gi:
                        name, per = freed[gi]
                        pe.wait_ge(S[name], per * (j + 1))
                    for c in range(CH):
                        last = mm(bank[j][:, 0:T], w[:, c, j * P:(j + 1) * P], xT[:, c, :],
                                  start=c == 0, stop=c == CH - 1)
                    last.then_inc(S["proj_done"], 1)
                    if gi == 0 and j == 0:
                        by_channel()
                    if gi == 2:
                        if j == 0:
                            pe.wait_ge(S["gatew_in"], 64)
                        gate_products(j)
                    if gi == 4 and j == 1:
                        pe.wait_ge(S["consts_ok"], 7)
                        sum_squares(0, "sqb_ok", "rmsb_psum")
            def out_product(t, banks, grp, s):
                t0, n = TILES[t]
                sides = [(h_, c) for h_ in range(2) for c in range(CT)] if t < 2 else \
                    [(h_, c) for c in range(CT) for h_ in range(2)]
                for h_, c in sides:
                    out = bank[banks[h_]][0:n, :] if t < 2 else bank[banks[h_]][UT * h_:UT * h_ + UT, :]
                    last = mm(out, mixT[:, grp * CT + c, t0:t0 + n], slot(s)[:, c, h_ * 512:(h_ + 1) * 512],
                              start=c == 0, stop=c == CT - 1, skip_group_check=t == 2)
                return last

            pe.wait_ge(S["yb_ok"], 1)
            pe.wait_ge(slot_loaded[5], 32)
            pe.wait_ge(S["sig_ok"], CT)
            for t in range(3):
                if t:
                    pe.wait_ge(S["bank_dve"], CT)
                    pe.wait_ge(S["plain_ok"], CT)
                if t == 1:
                    sum_squares(3, "sqa_ok", "rmsa_psum")
                out_product(t, LRU_BANKS[t], 1, 5).then_inc(S["lru_psum"], 1)
            pe.wait_ge(slot_loaded[3], 48)
            for t in range(3):
                if t:
                    pe.wait_ge(S["lru_left"], (None, 1, 3)[t])
                out_product(t, CONV_BANKS[t], 0, 3).then_inc(S["out_psum"], 1)
                if t == 0:
                    pe.wait_ge(S["states_ok"], 1)
                    pe.wait_ge(S["lru_left"], 2)
                    for j in range(CT):
                        last = nc.tensor.transpose(bank[6][0:OUTS, j * P:(j + 1) * P], states[:, j, 0:OUTS],
                                                   ident[:, :])
                    last.then_inc(S["states_psum"], 1)
            pe.wait_ge(S["router_in"], 32)
            for t, (t0, n) in enumerate(TILES):
                pe.wait_ge(x1_ok[t], 1)
                for c in range(CH):
                    b, col = ((2, 4)[t] + c // 4, (c % 4) * P) if t < 2 else (0, c * n)
                    last = nc.tensor.transpose(bank[b][:, col:col + n], x[0:n, t, c * P:(c + 1) * P],
                                               ident[0:n, 0:n])
                last.then_inc(S["x1t_psum"], 1)
                pe.wait_ge(S["x1t_dve"], t + 1)
                pe.wait_ge(S["x1t_act"], min(t + 1, 2))
                for c in range(CH):
                    last = mm(bank[LOGIT_BANKS[t]][0:n, 0:NE], xT[:, c, t0:t0 + n], router_w[:, c, :],
                              start=c == 0, stop=c == CH - 1)
                last.then_inc(S["logit_psum"], 1)
            pe.wait_ge(S["states_sb"], 1)
            pe.wait_ge(S["chosen_ok"], 3)
            for t, (t0, n) in enumerate(TILES):
                for t2 in range(t):
                    mm(bank[6][:, t * NE:(t + 1) * NE], ones_bf[:, :], chosen[:, t2, :],
                       start=t2 == 0, stop=False)
                mm(bank[6][:, t * NE:(t + 1) * NE], earlier_bf[0:n, :], chosen[0:n, t, :],
                   start=t == 0, stop=True)
            for t, (t0, n) in enumerate(TILES):
                last = mm(bank[6][:, 3 * NE:4 * NE], ones_bf[0:n, :], chosen[0:n, t, :],
                          start=t == 0, stop=t == 2)
            last.then_inc(S["rank_psum"], 1)
            pe.wait_ge(S["slot_hot_ok"], 2)
            pe.wait_ge(S["vals_ok"], 1)
            for t, (t0, n) in enumerate(TILES):
                for k in range(TOPK):
                    i = t * TOPK + k
                    last = mm(bank[7][:, 0:2 * TABW], slot_hot[0:n, i, :], unit_val[0:n, i, :],
                              start=i == 0, stop=i == 3 * TOPK - 1)
            last.then_inc(S["tab_psum"], 1)
            pe.wait_ge(S["expert_col_ok"], 1)
            mm(bank[2][0:1, 0:TABW], expert_col[0:TABW, :], ident[0:TABW, 0:TABW], start=True, stop=True)\
                .then_inc(S["expert_psum"], 1)

            def transposed(b, src, s):
                for c in range(4):
                    last = nc.tensor.transpose(bank[b][:, c * P:(c + 1) * P], src[:, c * P:(c + 1) * P], ident[:, :])
                last.then_inc(S[s], 1)

            pe.wait_ge(S["gathered"], 16)
            transposed(3, x_rows, "xu_psum")

            pe.wait_ge(S["tab_ok"], 1)
            n_unit = pe.value_load(units_through[0:1, NE - 1:NE], min_val=NE, max_val=MAXU)
            with pe.Fori(0, n_unit) as u:
                e = pe.value_load(unit_expert[0:1, bass.ds(u, 1)], min_val=0, max_val=NE - 1)

                def product(b, m, left, s):
                    for hf in range(2):
                        pe.wait_ge(slot_loaded[2 * m + hf], e * 16 + 16 * (PRIOR[2 * m + hf] + 1))
                        w = slot(2 * m + hf)
                        for c in range(4):
                            lhsT = left[:, c * P + hf * UT:c * P + hf * UT + UT]
                            end = hf == 1 and c == 3
                            for side in range(2):
                                last = mm(bank[b][side * UT:(side + 1) * UT, :], lhsT,
                                          w[:, c, side * HALF:(side + 1) * HALF], start=False, stop=end,
                                          skip_group_check=True)
                        if hf == 0:
                            last.then_inc(half_used[m], 1)
                    last.then_inc(S[s], 1)

                def biased(b, m):
                    return mm(bank[b][:, :], half_sel[:, :], bias_rows[:, m, :], start=True, stop=False,
                              skip_group_check=True)

                pe.wait_ge(S["xu_ok"], u + 1)
                pe.wait_ge(S["bias_in"], u * 48 + 48)
                pe.wait_ge(S["gate_free"], u + 1)
                biased(0, 0)
                product(0, 0, xTu, "gate_done")
                pe.wait_ge(S["up_free"], u + 1)
                biased(1, 1)
                product(1, 1, xTu, "up_done")
                pe.wait_ge(S["gathered"], u * 16 + 32)
                transposed(3, x_rows, "xu_psum")
                pe.wait_ge(S["y_ok"], u + 1)
                biased(2, 2).then_inc(S["bias_used"], 1)
                pe.wait_ge(S["hid_ok"], u + 1)
                transposed(4, hid, "hu_psum")
                pe.wait_ge(S["hu_ok"], u + 1)
                product(2, 2, hTu, "y_done")


_INS = ["x_prompt", "x_sample", "state_conv_a", "state_conv_b", "state_lru_h", "w_in", "conv_a_w", "conv_b_w",
        "conv_b_b", "lru_wa", "lru_ba", "lru_wi", "lru_bi", "lru_lambda", "gn_a", "gn_b", "w_out", "ln1_g", "ln1_b",
        "router_w", "router_b", "exp_w_gate", "exp_b_gate", "exp_w_up", "exp_b_up", "exp_w_down", "exp_b_down",
        "ln2_g", "ln2_b"]
_OUTS = [("y_prompt", (1, SEQ, D)), ("y_sample", (NB, DS, D)), ("prompt_conv_a", (1, 1, 2, CW)),
         ("prompt_conv_b", (1, 1, 3, CW)), ("prompt_lru_h", (1, 1, CW)), ("sample_conv_a", (1, NB, 2, CW)),
         ("sample_conv_b", (1, NB, 3, CW)), ("sample_lru_h", (1, NB, CW))]


def kernel(**inputs):
    import numpy as np
    import concourse.bacc as bacc
    from concourse.bass_utils import run_bass_kernel_spmd

    nc = bacc.Bacc("TRN2", target_bir_lowering=False, num_devices=1)
    arrays, args = {}, {}
    for name in _INS:
        v = np.ascontiguousarray(inputs[name])
        arrays[f"in_{name}"] = v
        args[name] = nc.dram_tensor(f"in_{name}", v.shape, mybir.dt.from_np(v.dtype), kind="ExternalInput").ap()
    for name, shape in _OUTS:
        args[name] = nc.dram_tensor(f"out_{name}", shape, mybir.dt.float32, kind="ExternalOutput").ap()
    hybrid_layer(nc, args)
    r = run_bass_kernel_spmd(nc, [arrays], core_ids=[0])
    return tuple(r.results[0][f"out_{name}"] for name, _ in _OUTS)
```

```python
import math
from contextlib import ExitStack

import concourse.bass as bass
from concourse import mybir

P = 128
D = 1024
CH = D // P
SEQ = 256
NB, DS = 8, 8
T = SEQ + NB * DS
TILES = [(0, 128), (128, 128), (256, 64)]
CW = 512
CT = CW // P
HIST = 3
SEG = HIST + DS
S0 = HIST + SEQ
FW = S0 + NB * SEG
OW = FW - HIST
NE, TOPK = 32, 4
UT = 64
MAXU = NE + T * TOPK // UT
TABW = MAXU + 2
HALF = D // 2
SLOTW = 4 * D
NSLOT = 6
ALPHA = 2.0 ** 0.25
LIMIT, SWISH = 7.0, 1.702
LN_EPS, RMS_EPS = 1e-5, 1e-6
LRU_C = 8.0
GELU_A, GELU_B = 0.044715, math.sqrt(2.0 / math.pi)

ROW_WA, ROW_WB, ROW_CB, ROW_BA, ROW_BI, ROW_LAM, ROW_GA, ROW_GB = 0, 3, 7, 8, 9, 10, 11, 12
ROW_SA, ROW_SB, ROW_H0, ROWS = 13, 29, 53, 61
OUT_PA, OUT_PB, OUT_PH, OUT_SA, OUT_SB, OUT_SH, OUTS = 0, 2, 5, 6, 22, 46, 54

IN_GROUPS = [(3, 3), (4, 4), (2, 5), (0, 3), (1, 4)]
LRU_BANKS = [(4, 5), (6, 1), (0, 0)]
CONV_BANKS = [(2, 3), (4, 5), (0, 0)]
LOGIT_BANKS = [1, 7, 3]
SUM_BANKS = [(5, 6), (7, 4), (1, 1)]
SUM_ORDER = (0, 2, 1)
PRIOR = [0, 0, 0, 3, 2, 2]


def hybrid_layer(nc, a):
    fp32, bf16 = mybir.dt.float32, mybir.dt.bfloat16
    i32, u32 = mybir.dt.int32, mybir.dt.uint32
    ALU, ACT, AX = mybir.AluOpType, mybir.ActivationFunctionType, mybir.AxisListType
    with ExitStack() as ctx:
        def sb(name, shape, dt=fp32):
            return ctx.enter_context(nc.sbuf_tensor(name, shape, dt))

        def sem(name):
            return ctx.enter_context(nc.semaphore(name))

        ring = sb("ring", [P, NSLOT, SLOTW])
        x = sb("x", [P, 3, D])
        xT = sb("xT", [P, CH, T])
        ident = sb("ident", [P, P])
        ones = sb("ones", [P, P])
        ones_bf = sb("ones_bf", [P, P], bf16)
        earlier_bf = sb("earlier_bf", [P, P], bf16)
        four_ident = sb("four_ident", [P, NE])
        half_sel = sb("half_sel", [2, P])
        part_sel = sb("part_sel", [66, P], bf16)
        zero_col = sb("zero_col", [34, 2])
        bias_parts = sb("bias_parts", [66, 2, HALF], bf16)
        iota_i = sb("iota_i", [P, P], i32)
        iota_e = sb("iota_e", [P, NE])
        unit_base = sb("unit_base", [P, TABW])
        unit_steps = sb("unit_steps", [P, T // UT - 1])
        iota_s = sb("iota_s", [P, UT])
        part_1 = sb("part_1", [P, 1])
        router_w = sb("router_w", [P, CH, NE])
        router_b = sb("router_b", [P, NE])
        ln_g = sb("ln_g", [P, D])
        ln_b = sb("ln_b", [P, D])
        stats = sb("stats", [P, 3, 12])
        mean_var = sb("mean_var", [P, 3, 2])
        rstd = sb("rstd", [P, 3])
        shift = sb("shift", [P, 3])
        unit_expert = sb("unit_expert", [1, TABW], i32)
        units_through = sb("units_through", [1, NE], i32)
        last_unit = sb("last_unit", [1, 1], i32)

        AREA = 15600
        area = sb("area", [P, AREA])
        at = [0]

        def carve(parts, *dims):
            n = math.prod(dims)
            v = area[0:parts, at[0]:at[0] + n]
            at[0] += n
            assert at[0] <= AREA, at[0]
            return v if len(dims) == 1 else v.rearrange("p (a b) -> p a b", b=dims[1])

        xl_pad = carve(P, CT, FW)
        cv_pad = carve(P, CT, FW)
        xc = carve(P, CT, OW)
        decay = carve(P, CT, OW)
        drive = carve(P, CT, OW)
        mult = carve(P, CT, OW)
        gate_c = carve(P, CT, T)
        gl = carve(P, CT, T)
        tmp = carve(P, CT, OW)
        conv_a = mult
        conv_gained = drive
        plain_a = decay
        params = carve(ROWS, CW)
        chan = carve(P, CT, 64)
        lam8 = carve(P, 2, CT)
        small = carve(P, 8, CT)
        wa_bd = carve(P, CT, P)
        wi_bd = carve(P, CT, P)
        rms = carve(P, 6)
        states = carve(P, CT, 64)
        states_out = carve(OUTS, CW)
        mixT = sb("mixT", [P, CH, T])
        at[0] = 0
        total = carve(P, 3, D)
        logit_part = carve(P, 3, P)
        logits = carve(P, 3, NE)
        top_v = carve(P, 3, 8)
        top_i = carve(P, 3, 8)
        top_f = carve(P, 3, TOPK)
        gates = carve(P, 3, TOPK)
        gsum = carve(P, 6)
        onehot = carve(P, 3, TOPK * NE)
        chosen_f = carve(P, 3, NE)
        more = carve(P, NE, T // UT - 1)
        n_more = carve(P, NE)
        ends = carve(P, NE + 1)
        pos = carve(P, 3, NE)
        place = carve(P, 3, NE)
        gate_of = carve(P, 3, NE)
        member = carve(P, 3, UT)
        gated = carve(P, 3, P)
        spread = carve(P, T)
        picked = carve(P, 3, TOPK * NE)
        ended = carve(P, NE)
        expert_col = carve(P, 1)
        x_rows = carve(P, HALF)
        xTu = carve(P, HALF)
        hTu = carve(P, HALF)
        g_min = carve(P, HALF)
        up_clip = carve(P, HALF)
        sig = carve(P, HALF)
        hid = carve(P, HALF)
        y_rows = carve(P, HALF)
        bias_rows = carve(34, 3, HALF)
        chosen = sb("chosen", [P, 3, NE], bf16)

        bank = [ctx.enter_context(nc.psum_tensor(f"bank{i}", [P, 512], fp32)) for i in range(8)]

        S = {n: sem(n) for n in (
            "first_cols params_in gatew_in router_in ln1_in ln2_in "
            "ident_ok four_ok consts_ok pads_ok bd_zero hist_ok "
            "xt_psum xt_dve chan_psum chan_ok lam_abs lam_exp lam_w lam_ln lam_ok "
            "proj_done xl_ok gl_ok c_ok bank_dve plain_ok xc_ok gates_psum sig_ok gelu_in gelu_t ath_ok one_m mult_ok "
            "x_scaled h_ok sqb_ok rmsb_psum rmsb_in rmsb_ok yb_ok conv_ok gained_ok sqa_ok rmsa_psum rmsa_in rmsa_ok "
            "cv_ok states_ok states_psum states_sb states_dma "
            "lru_psum lru_left out_psum resid_ok centred_ok var_ok rstd_ok shift_ok norm_ok scaled_ok "
            "x1t_psum x1t_act part_psum part_ok logit_psum top_ok exp_ok chosen_ok rank_psum "
            "expert_col_ok expert_psum tab_ok gu_bias_in gu_bias_used down_bias_in down_bias_used "
            "parts_zero sel_ok high_ok rest_ok mid_ok gu_split "
            "gate_done gate_free up_done up_free sig_done glu_ok hid_ok "
            "member_ok gathered rows_ok xu_psum xu_ok hu_psum hu_ok y_done y_ok "
            "gated_ok spread_psum spread_ok combined total_ok "
            "ln2_centred ln2_var ln2_rstd ln2_norm out_dma dve_step act_step pool_step").split()}
        slot_loaded = [sem(f"slot_loaded{i}") for i in range(NSLOT)]
        x_in, x1_ok, ln2_ok = ([sem(f"{n}{t}") for t in range(3)] for n in ("x_in", "x1_ok", "ln2_ok"))
        half_used = [sem(f"half_used{m}") for m in range(3)]
        product_done = ["gate_done", "up_done", "y_done"]

        block = ctx.enter_context(nc.Block())
        w_in_v = a["w_in"][0].rearrange("(c p) n -> p c n", p=P)
        w_out_v = a["w_out"][0].rearrange("(c p) n -> p c n", p=P)
        experts = [a["exp_w_gate"][0], a["exp_w_up"][0], a["exp_w_down"][0]]
        biases = [a["exp_b_gate"][0], a["exp_b_up"][0], a["exp_b_down"][0]]

        def slot_src(s, e):
            m = experts[s // 2]
            rows = m[e, (s % 2) * HALF:(s % 2 + 1) * HALF, :] if isinstance(e, int) else \
                m[bass.ds(e, 1), (s % 2) * HALF:(s % 2 + 1) * HALF, :].rearrange("o k n -> (o k) n")
            return rows.rearrange("(c p) n -> p c n", p=P)

        def slot(s):
            return ring[:, s, :].rearrange("p (c n) -> p c n", n=D)

        def sample_cols(v_, j):
            w_ = v_[:, j, S0:OW]
            return bass.AP(tensor=w_.tensor, offset=w_.offset, ap=[w_.ap[0], (SEG, NB), (1, DS)])

        @block.sync
        def _(sp):
            for t, (t0, n) in enumerate(TILES):
                src = a["x_prompt"][0, t0:t0 + n, :] if t < 2 else a["x_sample"].rearrange("b s d -> (b s) d")
                sp.dma_start(x[0:n, t, :], src).then_inc(x_in[t], 16)
            for i, (g, s) in enumerate(IN_GROUPS[:3]):
                first_col = g * CW
                if i == 0:
                    first_col += 2 * P
                    sp.dma_start(ring[:, s, :].rearrange("p (c n) -> p c n", n=CW)[:, :, 0:2 * P],
                                 w_in_v[:, :, g * CW:first_col]).then_inc(S["first_cols"], 16)
                if i == 1:
                    sp.wait_ge(S["params_in"], 16 * 11)
                sp.dma_start(ring[:, s, :].rearrange("p (c n) -> p c n", n=CW)[:, :, first_col - g * CW:CW],
                             w_in_v[:, :, first_col:(g + 1) * CW]).then_inc(slot_loaded[s], 16)
            for s in range(3):
                sp.dma_start(slot(s), slot_src(s, 0)).then_inc(slot_loaded[s], 16)
            for i, (g, s) in enumerate(IN_GROUPS[3:]):
                sp.wait_ge(S["proj_done"], CT * (i + 1))
                sp.dma_start(ring[:, s, :].rearrange("p (c n) -> p c n", n=CW),
                             w_in_v[:, :, g * CW:(g + 1) * CW]).then_inc(slot_loaded[s], 16)
            sp.wait_ge(S["proj_done"], 3 * CT)
            sp.dma_start(slot(5), w_out_v[:, CT:CH, :]).then_inc(slot_loaded[5], 16)
            sp.wait_ge(S["proj_done"], 4 * CT)
            sp.dma_start(slot(3), w_out_v[:, 0:CT, :]).then_inc(slot_loaded[3], 16)
            for s, done, count in ((4, "proj_done", 5 * CT), (5, "lru_psum", 3), (3, "out_psum", 3)):
                sp.wait_ge(S[done], count)
                sp.dma_start(slot(s), slot_src(s, 0)).then_inc(slot_loaded[s], 16)
            for t in range(3):
                sp.wait_ge(x1_ok[t], 1)
            for v, name in ((ln_g, "ln2_g"), (ln_b, "ln2_b")):
                sp.dma_start(v[:, :], a[name].partition_broadcast(P).rearrange("p o n -> p (o n)"))\
                    .then_inc(S["ln2_in"], 16)
            sp.wait_ge(S["tab_ok"], 1)

            def expert_load(e, before):
                used = sp.value_load(units_through[0:1, before], min_val=1, max_val=MAXU)
                for s in range(NSLOT):
                    sp.wait_ge(half_used[s // 2] if s % 2 == 0 else S[product_done[s // 2]], used)
                    sp.dma_start(slot(s), slot_src(s, e)).then_inc(slot_loaded[s], 16)

            expert_load(1, slice(0, 1))
            with sp.Fori(2, NE) as e:
                expert_load(e, bass.ds(e - 1, 1))
            for t in (1, 0, 2):
                t0, n = TILES[t]
                sp.wait_ge(ln2_ok[t], 1)
                dst = a["y_prompt"][0, t0:t0 + n, :] if t < 2 else a["y_sample"].rearrange("b s d -> (b s) d")
                sp.dma_start(dst, total[0:n, t, :]).then_inc(S["out_dma"], 16)
            sp.wait_ge(S["out_dma"], 48)
            sp.wait_ge(S["states_dma"], 96)

        @block.gpsimd
        def _(pool):
            g = nc.gpsimd
            step = [0]

            def settle(ins):
                step[0] += 1
                ins.then_inc(S["pool_step"], 1)
                pool.wait_ge(S["pool_step"], step[0])

            settle(g.memset(ident[:, :], 0.0))
            g.affine_select(out=ident[:, :], in_=ident[:, :], compare_op=ALU.not_equal, fill=1.0, base=0,
                            pattern=[[-1, P]], channel_multiplier=1).then_inc(S["ident_ok"], 1)
            g.memset(ones[:, :], 1.0).then_inc(S["consts_ok"], 1)
            settle(g.memset(ones_bf[:, :], 1.0))
            g.affine_select(out=earlier_bf[:, :], in_=ones_bf[:, :], compare_op=ALU.is_gt, fill=0.0, base=0,
                            pattern=[[1, P]], channel_multiplier=-1).then_inc(S["consts_ok"], 1)
            pool.wait_ge(S["consts_ok"], 2)
            settle(g.affine_select(out=half_sel[:, :], in_=ones[0:2, :], compare_op=ALU.is_ge, fill=0.0,
                                   base=0, pattern=[[1, P]], channel_multiplier=-UT))
            g.affine_select(out=half_sel[:, :], in_=half_sel[:, :], compare_op=ALU.is_ge, fill=0.0,
                            base=UT - 1, pattern=[[-1, P]], channel_multiplier=UT).then_inc(S["consts_ok"], 1)
            settle(g.iota(iota_i[:, :], pattern=[[1, P]], base=0, channel_multiplier=0))
            g.tensor_copy(iota_e[:, :], iota_i[:, 0:NE]).then_inc(S["consts_ok"], 1)
            g.tensor_copy(iota_s[:, :], iota_i[:, 0:UT]).then_inc(S["consts_ok"], 1)
            g.tensor_scalar(unit_steps[:, :], iota_i[:, 1:T // UT], UT, None, ALU.mult).then_inc(S["consts_ok"], 1)
            g.memset(bias_parts[:, :, :], 0.0).then_inc(S["parts_zero"], 1)
            g.memset(zero_col[:, :], 0.0)
            g.memset(part_sel[:, :], 0.0).then_inc(S["parts_zero"], 1)
            pool.wait_ge(S["parts_zero"], 2)
            pool.wait_ge(S["consts_ok"], 6)
            for i, p in enumerate((0, 32, 64)):
                g.tensor_copy(part_sel[p:p + 2, :], half_sel[:, :]).then_inc(S["sel_ok"], 1)
                pool.wait_ge(S["sel_ok"], i + 1)
            settle(g.iota(iota_i[:, 0:TABW], pattern=[[UT, TABW]], base=1, channel_multiplier=0))
            settle(g.tensor_copy(unit_base[:, :], iota_i[:, 0:TABW]))
            settle(g.iota(iota_i[:, 0:1], pattern=[[1, 1]], base=1, channel_multiplier=1))
            g.tensor_copy(part_1[:, :], iota_i[:, 0:1]).then_inc(S["consts_ok"], 1)
            pool.wait_ge(S["chan_ok"], 1)
            samples = slice(S0, FW)

            for j in range(CT):
                last = g.tensor_copy(
                    xl_pad[:, j, samples].rearrange("p (b s) -> p b s", s=SEG)[:, :, 0:3],
                    chan[:, j, ROW_SB:ROW_SB + 3 * NB].rearrange("p (b k) -> p b k", k=3))
                last = g.tensor_copy(
                    cv_pad[:, j, samples].rearrange("p (b s) -> p b s", s=SEG)[:, :, 1:3],
                    chan[:, j, ROW_SA:ROW_SA + 2 * NB].rearrange("p (b k) -> p b k", k=2))
                last.then_inc(S["hist_ok"], 1)
            def put(col, n, src):
                return g.tensor_copy(states[:, :, col:col + n], src)

            def put_samples(j, col, n, src, first_col):
                return g.tensor_copy(
                    states[:, j, col:col + n * NB].rearrange("p (b k) -> p b k", k=n),
                    src.rearrange("p (b s) -> p b s", s=SEG)[:, :, first_col:first_col + n])

            pool.wait_ge(S["xl_ok"], CT)
            put(OUT_PB, 3, xl_pad[:, :, S0 - 3:S0])
            for j in range(CT):
                put_samples(j, OUT_SB, 3, xl_pad[:, j, samples], SEG - 3)
            pool.wait_ge(S["h_ok"], 1)
            put(OUT_PH, 1, xc[:, :, SEQ - 1:SEQ])
            for j in range(CT):
                g.tensor_copy(states[:, j, OUT_SH:OUT_SH + NB], xc[:, j, S0 + DS - 1:OW:SEG])
            pool.wait_ge(S["cv_ok"], 4 * 2)
            put(OUT_PA, 2, cv_pad[:, :, S0 - 2:S0])
            for j in range(CT):
                last = put_samples(j, OUT_SA, 2, cv_pad[:, j, samples], SEG - 2)
            last.then_inc(S["states_ok"], 1)

            pool.wait_ge(S["ln1_in"], 32)
            pool.wait_ge(S["norm_ok"], 1)
            settle(g.tensor_tensor(x[:, 0, :], x[:, 0, :], ln_g[:, :], ALU.mult))
            g.tensor_tensor(x[:, 0, :], x[:, 0, :], ln_b[:, :], ALU.add).then_inc(x1_ok[0], 1)

            def bias_load(e, m, s):
                src = biases[m][e, :].rearrange("(h n) -> h n", h=2) if isinstance(e, int) else \
                    biases[m][bass.ds(e, 1), :].rearrange("o (h n) -> (o h) n", h=2)
                pool.dma_start(bias_rows[0:2, m, :], src).then_inc(S[s], 16)

            pool.wait_ge(S["states_dma"], 96)

            def load_gu(e):
                bias_load(e, 0, "gu_bias_in")
                bias_load(e, 1, "gu_bias_in")

            def split(count, next_expert=None):
                zero = zero_col[0:2, :].unsqueeze(2).to_broadcast([2, 2, HALF])
                zero_32 = zero_col[32:34, :].unsqueeze(2).to_broadcast([2, 2, HALF])
                whole, rest = bias_rows[0:2, 0:2, :], bias_rows[32:34, 0:2, :]
                g.tensor_tensor(bias_parts[0:2, :, :], whole, zero, ALU.add).then_inc(S["high_ok"], 1)
                pool.wait_ge(S["parts_zero"], 2)
                pool.wait_ge(S["high_ok"], count)
                g.tensor_tensor(rest, whole, bias_parts[0:2, :, :], ALU.subtract).then_inc(S["rest_ok"], 1)
                pool.wait_ge(S["parts_zero"], 2)
                pool.wait_ge(S["rest_ok"], count)
                if next_expert is not None:
                    load_gu(next_expert)
                g.tensor_tensor(bias_parts[32:34, :, :], rest, zero_32, ALU.add).then_inc(S["mid_ok"], 1)
                pool.wait_ge(S["parts_zero"], 2)
                pool.wait_ge(S["mid_ok"], count)
                g.tensor_tensor(bias_parts[64:66, :, :], rest, bias_parts[32:34, :, :], ALU.subtract)\
                    .then_inc(S["gu_split"], 1)

            load_gu(0)
            bias_load(0, 2, "down_bias_in")
            pool.wait_ge(S["gu_bias_in"], 32)
            split(1)
            pool.wait_ge(S["tab_ok"], 1)
            n_unit = pool.value_load(units_through[0:1, NE - 1:NE], min_val=NE, max_val=MAXU)
            e = pool.value_load(unit_expert[0:1, 1:2], min_val=0, max_val=NE - 1)
            pool.wait_ge(S["gu_split"], 1)
            load_gu(e)
            with pool.Fori(0, n_unit) as u:
                e_down = pool.value_load(unit_expert[0:1, bass.ds(u + 1, 1)], min_val=0, max_val=NE - 1)
                e_gu = pool.value_load(unit_expert[0:1, bass.ds(u + 2, 1)], min_val=0, max_val=NE - 1)
                gu_in, used, splits = pool.to_reg(u * 32 + 64), pool.to_reg(u + 1), pool.to_reg(u + 2)
                pool.wait_ge(S["tab_ok"], 1)
                pool.wait_ge(S["gu_bias_in"], gu_in)
                pool.wait_ge(S["gu_bias_used"], used)
                split(splits, e_gu)
                pool.wait_ge(S["tab_ok"], 1)
                pool.wait_ge(S["down_bias_used"], used)
                bias_load(e_down, 2, "down_bias_in")
            pool.wait_ge(S["gu_split"], n_unit + 1)
            pool.wait_ge(S["gu_bias_in"], n_unit * 32 + 64)
            pool.wait_ge(S["down_bias_in"], n_unit * 16 + 16)
            pool.wait_ge(S["ln2_in"], 32)
            pool.wait_ge(S["ln2_norm"], 1)
            settle(g.tensor_tensor(total[:, 0, :], total[:, 0, :], ln_g[:, :], ALU.mult))
            g.tensor_tensor(total[:, 0, :], total[:, 0, :], ln_b[:, :], ALU.add).then_inc(ln2_ok[0], 1)

        @block.scalar
        def _(act):
            s_ = nc.scalar
            step = [0]

            def settle(ins):
                step[0] += 1
                ins.then_inc(S["act_step"], 1)
                act.wait_ge(S["act_step"], step[0])

            for row, name, n in ((ROW_WA, "conv_a_w", 3), (ROW_WB, "conv_b_w", 4)):
                act.dma_start(params[row:row + n, :], a[name][0]).then_inc(S["params_in"], 16)
            for row, name in ((ROW_CB, "conv_b_b"), (ROW_BA, "lru_ba"), (ROW_BI, "lru_bi"), (ROW_LAM, "lru_lambda"),
                              (ROW_GA, "gn_a"), (ROW_GB, "gn_b")):
                act.dma_start(params[row:row + 1, :], a[name]).then_inc(S["params_in"], 16)
            act.dma_start(params[ROW_SA:ROW_SB, :], a["state_conv_a"][0].rearrange("b k c -> (b k) c"))\
                .then_inc(S["params_in"], 16)
            act.dma_start(params[ROW_SB:ROW_H0, :], a["state_conv_b"][0].rearrange("b k c -> (b k) c"))\
                .then_inc(S["params_in"], 16)
            act.dma_start(params[ROW_H0:ROWS, :], a["state_lru_h"][0]).then_inc(S["params_in"], 16)
            act.wait_ge(S["bd_zero"], 1)
            for dst, name in ((wa_bd, "lru_wa"), (wi_bd, "lru_wi")):
                for odd in range(2):
                    act.dma_start(dst[64 * odd:64 * odd + 64, :, 64 * odd:64 * odd + 64],
                                  a[name][0].rearrange("(j two) i o -> two i j o", two=2)[odd])\
                        .then_inc(S["gatew_in"], 16)
            act.dma_start(router_w[:, :, :], a["router_w"][0].rearrange("(c p) e -> p c e", p=P))\
                .then_inc(S["router_in"], 16)
            act.dma_start(router_b[:, :], a["router_b"].partition_broadcast(P).rearrange("p o n -> p (o n)"))\
                .then_inc(S["router_in"], 16)
            for v, name in ((ln_g, "ln1_g"), (ln_b, "ln1_b")):
                act.dma_start(v[:, :], a[name].partition_broadcast(P).rearrange("p o n -> p (o n)"))\
                    .then_inc(S["ln1_in"], 16)
            act.wait_ge(S["lam_abs"], 1)
            s_.activation(small[:, 1, :], small[:, 0, :], ACT.Exp, scale=-1.0).then_inc(S["lam_exp"], 1)
            act.wait_ge(S["lam_w"], 1)
            s_.activation(small[:, 3, :], small[:, 2, :], ACT.Ln).then_inc(S["lam_ln"], 1)
            for j in range(CT):
                act.wait_ge(S["proj_done"], j + 1)
                s_.copy(xl_pad[:, j, HIST:S0], bank[j][:, 0:SEQ])
                s_.copy(xl_pad[:, j, S0:FW].rearrange("p (b s) -> p b s", s=SEG)[:, :, HIST:SEG],
                        bank[j][:, SEQ:T].rearrange("p (b s) -> p b s", s=DS)).then_inc(S["xl_ok"], 1)
            for j in range(CT):
                act.wait_ge(S["proj_done"], CT + j + 1)
                s_.copy(gl[:, j, :], bank[j][:, 0:T]).then_inc(S["gl_ok"], 1)
            def gate_sigmoids(j):
                act.wait_ge(S["gates_psum"], j + 1)
                s_.activation(decay[:, j, :], bank[4][:, 0:OW], ACT.Sigmoid, bias=chan[:, j, ROW_BA:ROW_BA + 1])
                s_.activation(drive[:, j, :], bank[5][:, 0:OW], ACT.Sigmoid, bias=chan[:, j, ROW_BI:ROW_BI + 1])\
                    .then_inc(S["sig_ok"], 1)

            for j in range(CT):
                act.wait_ge(S["proj_done"], 2 * CT + j + 1)
                s_.copy(gate_c[:, j, :], bank[j][:, 0:T]).then_inc(S["c_ok"], 1)
                gate_sigmoids(j)
            act.wait_ge(S["gelu_in"], 1)
            s_.activation(tmp[:, :, 0:T], tmp[:, :, 0:T], ACT.Tanh, scale=GELU_B).then_inc(S["gelu_t"], 1)
            act.wait_ge(S["lam_ok"], 1)
            act.wait_ge(S["sig_ok"], CT)
            for j in range(CT):
                settle(s_.activation(mult[:, j, :], decay[:, j, :], ACT.Tanh, scale=lam8[:, 1, j:j + 1]))
                s_.activation(decay[:, j, :], decay[:, j, :], ACT.Exp, scale=lam8[:, 0, j:j + 1])\
                    .then_inc(S["ath_ok"], 1)
            act.wait_ge(S["one_m"], 1)
            s_.activation(mult, mult, ACT.Sqrt).then_inc(S["mult_ok"], 1)
            act.wait_ge(S["xt_psum"], 3)
            for t, (t0, n) in enumerate(TILES):
                last = s_.mul(x[0:n, t, :], x[0:n, t, :], ALPHA)
            last.then_inc(S["x_scaled"], 1)
            act.wait_ge(S["sqb_ok"], 1)
            for j in range(CT):
                last = s_.mul(mixT[:, CT + j, :], mixT[:, CT + j, :], chan[:, j, ROW_GB:ROW_GB + 1])
            last.then_inc(S["yb_ok"], 1)
            for j in range(CT):
                act.wait_ge(S["conv_ok"], j + 1)
                s_.mul(conv_gained[:, j, :], conv_a[:, j, :], chan[:, j, ROW_GA:ROW_GA + 1])\
                    .then_inc(S["gained_ok"], 1)
            act.wait_ge(S["rmsb_in"], 1)
            s_.activation(rms[:, 0:2], rms[:, 0:2], ACT.Sqrt)
            s_.activation(rms[0:UT, 2:3], rms[0:UT, 2:3], ACT.Sqrt).then_inc(S["rmsb_ok"], 1)
            act.wait_ge(S["plain_ok"], CT)
            s_.activation(tmp[:, :, 0:T], plain_a[:, :, 0:T], ACT.Square).then_inc(S["sqa_ok"], 1)
            act.wait_ge(S["rmsa_in"], 1)
            s_.activation(rms[:, 3:5], rms[:, 3:5], ACT.Sqrt)
            s_.activation(rms[0:UT, 5:6], rms[0:UT, 5:6], ACT.Sqrt).then_inc(S["rmsa_ok"], 1)
            act.wait_ge(S["states_psum"], 1)
            s_.copy(states_out, bank[6][0:OUTS, :]).then_inc(S["states_sb"], 1)
            act.wait_ge(S["states_sb"], 1)
            for name, col, n in (("prompt_conv_a", OUT_PA, 2), ("prompt_conv_b", OUT_PB, 3),
                                 ("prompt_lru_h", OUT_PH, 1),
                                 ("sample_conv_a", OUT_SA, 16), ("sample_conv_b", OUT_SB, 24),
                                 ("sample_lru_h", OUT_SH, 8)):
                dst = a[name][0]
                if "conv" in name:
                    dst = dst.rearrange("b k c -> (b k) c")
                act.dma_start(dst, states_out[col:col + n, :]).then_inc(S["states_dma"], 16)
            def x1t(t):
                act.wait_ge(S["x1t_psum"], t + 1)
                if t < 2:
                    for h_ in range(2):
                        last = s_.copy(xT[:, 4 * h_:4 * h_ + 4, t * P:(t + 1) * P],
                                       bank[((2, 3), (4, 5))[t][h_]][:, :].rearrange("p (c n) -> p c n", c=4))
                else:
                    last = s_.copy(xT[:, :, 2 * P:T], bank[0][:, :].rearrange("p (c n) -> p c n", c=CH))
                last.then_inc(S["x1t_act"], 1)

            def logit_parts(t):
                n = TILES[t][1]
                act.wait_ge(S["part_psum"], t + 1)
                s_.copy(logit_part[:, t, 0:n], bank[LOGIT_BANKS[t]][:, 0:n]).then_inc(S["part_ok"], 1)

            for t, (t0, n) in enumerate(TILES):
                act.wait_ge(S["var_ok"], t + 1)
                s_.activation(rstd[0:n, t:t + 1], rstd[0:n, t:t + 1], ACT.Sqrt).then_inc(S["rstd_ok"], 1)
                if t == 0:
                    act.wait_ge(S["shift_ok"], 1)
                    s_.activation(x[:, 0, :], x[:, 0, :], ACT.Identity, bias=shift[:, 0:1],
                                  scale=rstd[:, 0:1]).then_inc(S["norm_ok"], 1)
                if t == 1:
                    x1t(0)
            logit_parts(0)
            x1t(1)
            logit_parts(1)
            x1t(2)
            logit_parts(2)
            for t, (t0, n) in enumerate(TILES):
                act.wait_ge(S["top_ok"], t + 1)
                s_.activation(gates[0:n, t, :], top_v[0:n, t, 0:TOPK], ACT.Exp, bias=gsum[0:n, t:t + 1],
                              accum_out=gsum[0:n, 3 + t:4 + t]).then_inc(S["exp_ok"], 1)
            for t, (t0, n) in enumerate(TILES):
                act.wait_ge(x1_ok[t], 1)
                s_.mul(total[0:n, t, :], x[0:n, t, :], ALPHA).then_inc(S["scaled_ok"], 1)
            act.wait_ge(S["gathered"], 1)
            s_.copy(x_rows, bank[3][:, :]).then_inc(S["rows_ok"], 1)
            act.wait_ge(S["xu_psum"], 1)
            s_.copy(xTu, bank[3][:, :]).then_inc(S["xu_ok"], 1)

            act.wait_ge(S["tab_ok"], 1)
            n_unit = act.value_load(units_through[0:1, NE - 1:NE], min_val=NE, max_val=MAXU)
            with act.Fori(0, n_unit) as u:
                act.wait_ge(S["gate_free"], u + 2)
                s_.activation(sig, g_min, ACT.Sigmoid, scale=SWISH).then_inc(S["sig_done"], 1)
                act.wait_ge(S["spread_psum"], u + 1)
                s_.copy(spread, bank[5][:, 0:T]).then_inc(S["spread_ok"], 1)
                act.wait_ge(S["gathered"], u + 2)
                s_.copy(x_rows, bank[3][:, :]).then_inc(S["rows_ok"], 1)
                act.wait_ge(S["hu_psum"], u + 1)
                s_.copy(hTu, bank[4][:, :]).then_inc(S["hu_ok"], 1)
                act.wait_ge(S["xu_psum"], u + 2)
                s_.copy(xTu, bank[3][:, :]).then_inc(S["xu_ok"], 1)
                act.wait_ge(S["y_done"], u + 1)
                s_.copy(y_rows, bank[2][:, :]).then_inc(S["y_ok"], 1)

            for t, (t0, n) in enumerate(TILES):
                act.wait_ge(S["ln2_var"], t + 1)
                s_.activation(rstd[0:n, t:t + 1], rstd[0:n, t:t + 1], ACT.Sqrt).then_inc(S["ln2_rstd"], 1)
                if t == 0:
                    act.wait_ge(S["shift_ok"], 2)
                    s_.activation(total[:, 0, :], total[:, 0, :], ACT.Identity, bias=shift[:, 0:1],
                                  scale=rstd[:, 0:1]).then_inc(S["ln2_norm"], 1)

        @block.vector
        def _(dve):
            v = nc.vector
            step = [0]

            def settle(ins):
                step[0] += 1
                ins.then_inc(S["dve_step"], 1)
                dve.wait_ge(S["dve_step"], step[0])

            v.memset(wa_bd, 0.0)
            v.memset(wi_bd, 0.0).then_inc(S["bd_zero"], 1)
            v.memset(xl_pad[:, :, 0:HIST], 0.0)
            v.memset(cv_pad[:, :, 0:HIST], 0.0)
            v.memset(cv_pad[:, :, S0:FW].rearrange("p c (b s) -> p c b s", s=SEG)[:, :, :, 0], 0.0)\
                .then_inc(S["pads_ok"], 1)
            dve.wait_ge(S["ident_ok"], 1)
            v.reduce_sum(four_ident[:, :], ident[:, :].rearrange("p (j e) -> p e j", e=NE), AX.X)\
                .then_inc(S["four_ok"], 1)
            for t in range(3):
                dve.wait_ge(S["xt_psum"], t + 1)
                if t < 2:
                    for h_ in range(2):
                        last = v.tensor_copy(xT[:, 4 * h_:4 * h_ + 4, t * P:(t + 1) * P],
                                             bank[2 * t + h_][:, :].rearrange("p (c n) -> p c n", c=4))
                else:
                    last = v.tensor_copy(xT[:, :, 2 * P:T], bank[4][:, :].rearrange("p (c n) -> p c n", c=CH))
                last.then_inc(S["xt_dve"], 1)
            dve.wait_ge(S["chan_psum"], 1)
            v.tensor_copy(chan[:, :, 0:ROWS], bank[6][:, 0:CT * 64].rearrange("p (c n) -> p c n", c=CT)[:, :, 0:ROWS])\
                .then_inc(S["chan_ok"], 1)
            dve.wait_ge(S["chan_ok"], 1)
            lam = chan[:, :, ROW_LAM]
            ab, q, w, lnw, d, rec, res, extra = (small[:, i, :] for i in range(8))
            v.scalar_tensor_tensor(ab, lam, -1.0, lam, ALU.mult, ALU.max).then_inc(S["lam_abs"], 1)
            dve.wait_ge(S["lam_exp"], 1)
            v.tensor_scalar(w, q, 1.0, None, ALU.add).then_inc(S["lam_w"], 1)
            dve.wait_ge(S["lam_w"], 1)
            settle(v.tensor_scalar(d, w, -1.0, None, ALU.add))
            settle(v.tensor_scalar(rec, d, 1e-30, None, ALU.max))
            settle(v.reciprocal(rec, rec))
            settle(v.tensor_tensor(rec, rec, q, ALU.mult))
            settle(v.tensor_scalar(extra, d, 0.0, None, ALU.is_equal))
            settle(v.tensor_tensor(extra, extra, q, ALU.mult))
            dve.wait_ge(S["lam_ln"], 1)
            settle(v.tensor_tensor(res, lnw, rec, ALU.mult))
            settle(v.tensor_tensor(res, res, extra, ALU.add))
            settle(v.tensor_scalar(extra, lam, -1.0, 0.0, ALU.mult, ALU.max))
            settle(v.tensor_tensor(res, res, extra, ALU.add))
            v.tensor_scalar(lam8[:, 0, :], res, -LRU_C, None, ALU.mult)
            v.tensor_scalar(lam8[:, 1, :], res, LRU_C, None, ALU.mult).then_inc(S["lam_ok"], 1)

            dve.wait_ge(S["hist_ok"], CT)
            dve.wait_ge(S["pads_ok"], 1)
            for j in range(CT):
                dve.wait_ge(S["xl_ok"], j + 1)
                settle(v.tensor_scalar(xc[:, j, :], xl_pad[:, j, 0:OW], chan[:, j, ROW_WB:ROW_WB + 1],
                                       chan[:, j, ROW_CB:ROW_CB + 1], ALU.mult, ALU.add))
                for k in range(1, 4):
                    last = v.scalar_tensor_tensor(xc[:, j, :], xl_pad[:, j, k:k + OW],
                                                  chan[:, j, ROW_WB + k:ROW_WB + k + 1], xc[:, j, :],
                                                  ALU.mult, ALU.add)
                    if k < 3:
                        settle(last)
                last.then_inc(S["xc_ok"], 1)
            arg = tmp[:, :, 0:T]
            dve.wait_ge(S["gl_ok"], CT)
            settle(v.tensor_tensor(arg, gl, gl, ALU.mult))
            settle(v.tensor_scalar(arg, arg, GELU_A, 1.0, ALU.mult, ALU.add))
            v.tensor_tensor(arg, arg, gl, ALU.mult).then_inc(S["gelu_in"], 1)
            dve.wait_ge(S["gelu_t"], 1)
            settle(v.scalar_tensor_tensor(gl, arg, 1.0, gl, ALU.add, ALU.mult))

            def masked_v(j):
                dve.wait_ge(S["proj_done"], 3 * CT + j + 1)
                v.tensor_tensor(cv_pad[:, j, HIST:S0], bank[j][:, 0:SEQ], gate_c[:, j, 0:SEQ], ALU.mult)\
                    .then_inc(S["cv_ok"], 1)
                v.tensor_tensor(cv_pad[:, j, S0:FW].rearrange("p (b s) -> p b s", s=SEG)[:, :, HIST:SEG],
                                bank[j][:, SEQ:T].rearrange("p (b s) -> p b s", s=DS),
                                gate_c[:, j, SEQ:T].rearrange("p (b s) -> p b s", s=DS), ALU.mult)\
                    .then_inc(S["cv_ok"], 1)

            dve.wait_ge(S["ath_ok"], CT)
            settle(v.tensor_tensor(tmp, decay, decay, ALU.mult))
            v.scalar_tensor_tensor(mult, tmp, 1.0, mult, ALU.add, ALU.mult).then_inc(S["one_m"], 1)
            settle(v.tensor_tensor(drive, drive, xc, ALU.mult))
            dve.wait_ge(S["c_ok"], CT)
            masked_v(0)
            dve.wait_ge(S["mult_ok"], 1)
            settle(v.tensor_tensor(drive, drive, mult, ALU.mult))
            for j in range(CT):
                v.memset(decay[:, j, 0:1], 0.0)
                v.memset(decay[:, j, S0 - 1:OW:SEG], 0.0)
                last = v.tensor_copy(drive[:, j, S0 - 1:OW:SEG], chan[:, j, ROW_H0:ROW_H0 + NB])
            settle(last)
            h = xc.rearrange("p c w -> p (c w)")
            v.tensor_tensor_scan(h, decay.rearrange("p c w -> p (c w)"), drive.rearrange("p c w -> p (c w)"),
                                 0.0, ALU.mult, ALU.add).then_inc(S["h_ok"], 1)
            masked_v(1)
            dve.wait_ge(S["h_ok"], 1)
            settle(v.scalar_tensor_tensor(mixT[:, CT:CH, 0:SEQ], gl[:, :, 0:SEQ], 0.5, xc[:, :, 0:SEQ],
                                          ALU.mult, ALU.mult))
            for j in range(CT):
                last = v.scalar_tensor_tensor(
                    mixT[:, CT + j, SEQ:T].rearrange("p (b s) -> p b s", s=DS),
                    gl[:, j, SEQ:T].rearrange("p (b s) -> p b s", s=DS), 0.5,
                    sample_cols(xc, j), ALU.mult, ALU.mult)
            settle(last)
            sq = tmp[:, :, 0:T]
            v.tensor_tensor(sq, mixT[:, CT:CH, :], mixT[:, CT:CH, :], ALU.mult).then_inc(S["sqb_ok"], 1)

            def conv_a_tile(j):
                dve.wait_ge(S["cv_ok"], 2 * (j + 1))
                settle(v.tensor_scalar(conv_a[:, j, :], cv_pad[:, j, 1:1 + OW], chan[:, j, ROW_WA:ROW_WA + 1],
                                       None, ALU.mult))
                for k in range(1, 3):
                    last = v.scalar_tensor_tensor(conv_a[:, j, :], cv_pad[:, j, 1 + k:1 + k + OW],
                                                  chan[:, j, ROW_WA + k:ROW_WA + k + 1], conv_a[:, j, :],
                                                  ALU.mult, ALU.add)
                    if k == 1:
                        settle(last)
                last.then_inc(S["conv_ok"], 1)

            def gated_a(j):
                dve.wait_ge(S["proj_done"], 4 * CT + j + 1)
                dve.wait_ge(S["gained_ok"], j + 1)
                for dst, conv, s in ((mixT[:, j, :], conv_gained, "bank_dve"),
                                     (plain_a[:, j, 0:T], conv_a, "plain_ok")):
                    v.tensor_tensor(dst[:, 0:SEQ], bank[j][:, 0:SEQ], conv[:, j, 0:SEQ], ALU.mult)
                    v.tensor_tensor(dst[:, SEQ:T].rearrange("p (b s) -> p b s", s=DS),
                                    bank[j][:, SEQ:T].rearrange("p (b s) -> p b s", s=DS), sample_cols(conv, j),
                                    ALU.mult).then_inc(S[s], 1)

            masked_v(2)
            masked_v(3)
            for j in range(CT):
                conv_a_tile(j)

            def inv_rms_in(col, s):
                for n, c0, c1 in ((P, col, col + 2), (UT, col + 2, col + 3)):
                    last = v.tensor_scalar(rms[0:n, c0:c1], bank[7][0:n, c0:c1], 1.0 / CW, RMS_EPS, ALU.mult, ALU.add)
                settle(last)
                v.reciprocal(rms[:, col:col + 2], rms[:, col:col + 2])
                v.reciprocal(rms[0:UT, col + 2:col + 3], rms[0:UT, col + 2:col + 3]).then_inc(S[s], 1)

            gated_a(0)
            gated_a(1)
            dve.wait_ge(S["rmsb_psum"], 1)
            inv_rms_in(0, "rmsb_in")
            gated_a(2)
            gated_a(3)

            def add_product(t, banks, col, s):
                n = TILES[t][1]
                for h_ in range(2):
                    src = banks[h_][0:n, :] if t < 2 else banks[h_][UT * h_:UT * h_ + UT, :]
                    last = v.scalar_tensor_tensor(x[0:n, t, h_ * 512:(h_ + 1) * 512], src,
                                                  rms[0:n, col + t:col + t + 1],
                                                  x[0:n, t, h_ * 512:(h_ + 1) * 512], ALU.mult, ALU.add)
                last.then_inc(S[s], 1)

            dve.wait_ge(S["rmsb_ok"], 1)
            dve.wait_ge(S["x_scaled"], 1)
            for t in range(3):
                dve.wait_ge(S["lru_psum"], t + 1)
                add_product(t, [bank[i] for i in LRU_BANKS[t]], 0, "lru_left")
                if t == 0:
                    dve.wait_ge(S["rmsa_psum"], 1)
                    inv_rms_in(3, "rmsa_in")
            dve.wait_ge(S["rmsa_ok"], 1)

            def moments(src, t, n, s):
                v.bn_stats(stats[0:n, t, 0:6], src[0:n, t, 0:512])
                settle(v.bn_stats(stats[0:n, t, 6:12], src[0:n, t, 512:1024]))
                settle(v.bn_aggr(mean_var[0:n, t, :], stats[0:n, t, :].rearrange("p (a b) -> p a b", b=6)))
                settle(v.tensor_scalar(rstd[0:n, t:t + 1], mean_var[0:n, t, 1:2], LN_EPS, None, ALU.add))
                v.reciprocal(rstd[0:n, t:t + 1], rstd[0:n, t:t + 1]).then_inc(S[s], 1)

            def offset(t):
                v.scalar_tensor_tensor(shift[:, t:t + 1], mean_var[:, t, 0:1], -1.0, rstd[:, t:t + 1],
                                       ALU.mult, ALU.mult).then_inc(S["shift_ok"], 1)

            def affine(dst, t, n, centred, count, root, s):
                v.scalar_tensor_tensor(dst[0:n, t, :], dst[0:n, t, :], mean_var[0:n, t, 0:1], ln_g[0:n, :],
                                       ALU.subtract, ALU.mult).then_inc(S[centred], 1)
                dve.wait_ge(S[centred], count)
                dve.wait_ge(S[root], t + 1)
                v.scalar_tensor_tensor(dst[0:n, t, :], dst[0:n, t, :], rstd[0:n, t:t + 1], ln_b[0:n, :],
                                       ALU.mult, ALU.add).then_inc(s, 1)

            dve.wait_ge(S["ln1_in"], 32)

            def residual(t):
                n = TILES[t][1]
                dve.wait_ge(S["out_psum"], t + 1)
                dve.wait_ge(S["lru_left"], t + 1)
                add_product(t, [bank[i] for i in CONV_BANKS[t]], 3, "resid_ok")
                dve.wait_ge(S["resid_ok"], t + 1)
                moments(x, t, n, "var_ok")

            def best_experts(t):
                n = TILES[t][1]
                dve.wait_ge(S["logit_psum"], t + 1)
                settle(v.tensor_tensor(logits[0:n, t, :], bank[LOGIT_BANKS[t]][0:n, 0:NE], router_b[0:n, :], ALU.add))
                settle(v.max(top_v[0:n, t, :], logits[0:n, t, :]))
                v.tensor_scalar(gsum[0:n, t:t + 1], top_v[0:n, t, 0:1], -1.0, None, ALU.mult).then_inc(S["top_ok"], 1)
                settle(v.max_index(top_i[0:n, t, :].bitcast(u32), top_v[0:n, t, :], logits[0:n, t, :]))
                settle(v.tensor_copy(top_f[0:n, t, :], top_i[0:n, t, 0:TOPK].bitcast(u32)))
                hot = onehot[0:n, t, :].rearrange("p (k e) -> p k e", e=NE)
                settle(v.tensor_tensor(hot, iota_e[0:n, :].unsqueeze(1).to_broadcast([n, TOPK, NE]),
                                       top_f[0:n, t, :].unsqueeze(2).to_broadcast([n, TOPK, NE]), ALU.is_equal))
                settle(v.reduce_sum(chosen_f[0:n, t, :], hot.rearrange("p k e -> p e k"), AX.X))
                v.tensor_copy(chosen[0:n, t, :], chosen_f[0:n, t, :]).then_inc(S["chosen_ok"], 1)

            def normed_gates(t):
                n = TILES[t][1]
                dve.wait_ge(S["exp_ok"], t + 1)
                settle(v.reciprocal(gsum[0:n, 3 + t:4 + t], gsum[0:n, 3 + t:4 + t]))
                settle(v.tensor_scalar(gates[0:n, t, :], gates[0:n, t, :], gsum[0:n, 3 + t:4 + t], None, ALU.mult))

            residual(0)
            dve.wait_ge(S["states_ok"], 1)
            v.memset(ends[:, 0:1], 0.0)
            v.memset(gates[UT:P, 2, :], 0.0)
            v.memset(chosen_f[UT:P, 2, :], 0.0)
            settle(v.memset(onehot[UT:P, 2, :], 0.0))
            dve.wait_ge(S["rstd_ok"], 1)
            offset(0)
            residual(1)
            affine(x, 1, P, "centred_ok", 1, "rstd_ok", x1_ok[1])
            residual(2)
            affine(x, 2, UT, "centred_ok", 2, "rstd_ok", x1_ok[2])
            dve.wait_ge(S["router_in"], 32)
            best_experts(0)
            best_experts(1)
            best_experts(2)
            dve.wait_ge(S["rank_psum"], 1)
            counts = bank[6][:, 3 * NE:4 * NE]
            settle(v.tensor_tensor(more, counts.unsqueeze(2).to_broadcast([P, NE, T // UT - 1]),
                                   unit_steps[:, :].unsqueeze(1).to_broadcast([P, NE, T // UT - 1]), ALU.is_gt))
            settle(v.reduce_sum(n_more, more, AX.X))
            settle(v.tensor_tensor_scan(ends[:, 1:NE + 1], n_more, ones[:, 0:NE], 0.0, ALU.add, ALU.add))
            v.tensor_copy(units_through[:, :], ends[0:1, 1:NE + 1])
            v.tensor_scalar(last_unit[:, :], ends[0:1, NE:NE + 1], -1.0, None, ALU.add)
            v.tensor_scalar(ended, ends[:, 1:NE + 1], part_1[:, 0:1], None, ALU.is_lt)
            settle(v.scalar_tensor_tensor(pos, ends[:, 0:NE].unsqueeze(1).to_broadcast([P, 3, NE]), float(UT),
                                          bank[6][:, 0:3 * NE].rearrange("p (t e) -> p t e", e=NE),
                                          ALU.mult, ALU.add))
            v.reduce_sum(expert_col, ended, AX.X).then_inc(S["expert_col_ok"], 1)
            settle(v.scalar_tensor_tensor(place, pos, 1.0, chosen_f, ALU.add, ALU.mult))

            def members(e, u):
                for t in range(3):
                    last = v.tensor_scalar(member[:, t, :], iota_s[:, :], unit_base[:, u], place[:, t, e],
                                           ALU.add, ALU.is_equal)
                last.then_inc(S["member_ok"], 1)

            def gated_members(e):
                for t in range(3):
                    last = v.tensor_scalar(gated[:, t, :].rearrange("p (h s) -> p h s", h=2),
                                           member[:, t, :].unsqueeze(1).to_broadcast([P, 2, UT]),
                                           gate_of[:, t, e], None, ALU.mult)
                last.then_inc(S["gated_ok"], 1)

            members(slice(0, 1), slice(0, 1))
            for t in range(3):
                normed_gates(t)
            picks = picked.rearrange("p t (k e) -> p t k e", e=NE)
            settle(v.tensor_tensor(picks, onehot.rearrange("p t (k e) -> p t k e", e=NE),
                                   gates.unsqueeze(3).to_broadcast([P, 3, TOPK, NE]), ALU.mult))
            settle(v.reduce_sum(gate_of, picks.rearrange("p t k e -> p t e k"), AX.X))
            dve.wait_ge(S["member_ok"], 1)
            gated_members(slice(0, 1))
            dve.wait_ge(S["expert_psum"], 1)
            v.tensor_scalar(unit_expert[:, :], bank[7][0:1, 0:TABW], float(NE - 1), None, ALU.min)\
                .then_inc(S["tab_ok"], 1)

            dve.wait_ge(S["tab_ok"], 1)
            dve.wait_ge(S["scaled_ok"], 3)
            dve.sem_inc(S["gate_free"], 1)
            n_last = dve.value_load(last_unit[0:1, 0:1], min_val=NE - 1, max_val=MAXU - 1)

            def add_results(u, order, then=None):
                for i, t in enumerate(order):
                    n = TILES[t][1]
                    dve.wait_ge(S["combined"], u * 3 + (i + 1))
                    for h_ in range(2):
                        b = bank[SUM_BANKS[t][h_]]
                        src = b[0:n, :] if t < 2 else b[UT * h_:UT * h_ + UT, :]
                        cols = slice(h_ * HALF, (h_ + 1) * HALF)
                        last = v.tensor_tensor(total[0:n, t, cols], src, total[0:n, t, cols], ALU.add)
                    last.then_inc(S["total_ok"], 1)
                    if then:
                        dve.wait_ge(S["total_ok"], u * 3 + (i + 1))
                        then(t)

            def unit(u, next_expert, next_unit):
                dve.wait_ge(S["gate_done"], u + 1)
                v.tensor_scalar(g_min, bank[0][:, :], LIMIT, None, ALU.min).then_inc(S["gate_free"], 1)
                dve.wait_ge(S["gated_ok"], u + 1)
                members(next_expert, next_unit)
                dve.wait_ge(S["sig_done"], u + 1)
                v.tensor_tensor(g_min, g_min, sig, ALU.mult).then_inc(S["glu_ok"], 1)
                dve.wait_ge(S["up_done"], u + 1)
                v.tensor_scalar(up_clip, bank[1][:, :], LIMIT, -LIMIT, ALU.min, ALU.max).then_inc(S["up_free"], 1)
                dve.wait_ge(S["up_free"], u + 1)
                dve.wait_ge(S["glu_ok"], u + 1)
                v.scalar_tensor_tensor(hid, up_clip, 1.0, g_min, ALU.add, ALU.mult).then_inc(S["hid_ok"], 1)
                dve.wait_ge(S["spread_psum"], u + 1)
                dve.wait_ge(S["member_ok"], u + 2)
                gated_members(next_expert)

            second = dve.value_load(unit_expert[0:1, 1:2], min_val=0, max_val=NE - 1)
            unit(0, bass.ds(second, 1), slice(1, 2))
            with dve.Fori(0, n_last) as before:
                e = dve.value_load(unit_expert[0:1, bass.ds(before + 2, 1)], min_val=0, max_val=NE - 1)
                add_results(before, SUM_ORDER)
                unit(before + 1, bass.ds(e, 1), bass.ds(before + 2, 1))

            dve.wait_ge(S["ln2_in"], 32)

            def second_norm(t):
                moments(total, t, TILES[t][1], "ln2_var")
                if t == 0:
                    dve.wait_ge(S["ln2_rstd"], 1)
                    offset(0)
                else:
                    affine(total, t, TILES[t][1], "ln2_centred", t, "ln2_rstd", ln2_ok[t])

            add_results(n_last, (0, 1, 2), then=second_norm)

        @block.tensor
        def _(pe):
            mm = nc.tensor.matmul
            pe.wait_ge(S["ident_ok"], 1)
            for t, (t0, n) in enumerate(TILES):
                pe.wait_ge(x_in[t], 16)
                for c in range(CH):
                    b, col = (2 * t + c // 4, (c % 4) * P) if t < 2 else (4, c * n)
                    last = nc.tensor.transpose(bank[b][:, col:col + n], x[0:n, t, c * P:(c + 1) * P],
                                               ident[0:n, 0:n])
                last.then_inc(S["xt_psum"], 1)
            pe.wait_ge(S["xt_dve"], 3)

            def by_channel():
                pe.wait_ge(S["params_in"], 16 * 11)
                for j in range(CT):
                    last = nc.tensor.transpose(bank[6][:, j * 64:j * 64 + ROWS], params[:, j * P:(j + 1) * P],
                                               ident[0:ROWS, 0:ROWS])
                last.then_inc(S["chan_psum"], 1)

            def gate_products(j):
                pe.wait_ge(S["xc_ok"], j + 1)
                if j:
                    pe.wait_ge(S["sig_ok"], j)
                mm(bank[4][:, 0:OW], wa_bd[:, j, :], xc[:, j, :], start=True, stop=True)
                mm(bank[5][:, 0:OW], wi_bd[:, j, :], xc[:, j, :], start=True, stop=True)\
                    .then_inc(S["gates_psum"], 1)

            def sum_squares(col, ok, s):
                pe.wait_ge(S[ok], 1)
                for t, (t0, n) in enumerate(TILES):
                    for j in range(CT):
                        last = mm(bank[7][0:n, col + t:col + t + 1], tmp[:, j, t0:t0 + n], ones[:, 0:1],
                                  start=j == 0, stop=j == CT - 1)
                last.then_inc(S[s], 1)

            freed = {1: ("xl_ok", 1), 2: ("gl_ok", 1), 3: ("c_ok", 1), 4: ("cv_ok", 2)}
            seen = [0] * NSLOT
            for gi, (g, s) in enumerate(IN_GROUPS):
                seen[s] += 1
                w = ring[:, s, :].rearrange("p (c n) -> p c n", n=CW)
                for j in range(CT):
                    if gi == 0 and j == 0:
                        pe.wait_ge(S["first_cols"], 16)
                    elif j == (2 if gi == 0 else 0):
                        pe.wait_ge(slot_loaded[s], 16 * seen[s])
                    if gi:
                        name, per = freed[gi]
                        pe.wait_ge(S[name], per * (j + 1))
                    for c in range(CH):
                        last = mm(bank[j][:, 0:T], w[:, c, j * P:(j + 1) * P], xT[:, c, :],
                                  start=c == 0, stop=c == CH - 1)
                    last.then_inc(S["proj_done"], 1)
                    if gi == 0 and j == 0:
                        by_channel()
                    if gi == 2:
                        if j == 0:
                            pe.wait_ge(S["gatew_in"], 64)
                        gate_products(j)
                    if gi == 4 and j == 1:
                        pe.wait_ge(S["consts_ok"], 7)
                        sum_squares(0, "sqb_ok", "rmsb_psum")
            def out_product(t, banks, grp, s):
                t0, n = TILES[t]
                sides = [(h_, c) for h_ in range(2) for c in range(CT)] if t < 2 else \
                    [(h_, c) for c in range(CT) for h_ in range(2)]
                for h_, c in sides:
                    out = bank[banks[h_]][0:n, :] if t < 2 else bank[banks[h_]][UT * h_:UT * h_ + UT, :]
                    last = mm(out, mixT[:, grp * CT + c, t0:t0 + n], slot(s)[:, c, h_ * 512:(h_ + 1) * 512],
                              start=c == 0, stop=c == CT - 1, skip_group_check=t == 2)
                return last

            pe.wait_ge(S["yb_ok"], 1)
            pe.wait_ge(slot_loaded[5], 32)
            pe.wait_ge(S["sig_ok"], CT)
            for t in range(3):
                if t:
                    pe.wait_ge(S["bank_dve"], CT)
                    pe.wait_ge(S["plain_ok"], CT)
                if t == 1:
                    sum_squares(3, "sqa_ok", "rmsa_psum")
                out_product(t, LRU_BANKS[t], 1, 5).then_inc(S["lru_psum"], 1)
            pe.wait_ge(slot_loaded[3], 48)
            for t in range(3):
                if t:
                    pe.wait_ge(S["lru_left"], (None, 1, 3)[t])
                out_product(t, CONV_BANKS[t], 0, 3).then_inc(S["out_psum"], 1)
                if t == 0:
                    pe.wait_ge(S["states_ok"], 1)
                    pe.wait_ge(S["lru_left"], 2)
                    for j in range(CT):
                        last = nc.tensor.transpose(bank[6][0:OUTS, j * P:(j + 1) * P], states[:, j, 0:OUTS],
                                                   ident[:, :])
                    last.then_inc(S["states_psum"], 1)
            pe.wait_ge(S["router_in"], 32)
            pe.wait_ge(S["four_ok"], 1)
            def x1t(t):
                t0, n = TILES[t]
                pe.wait_ge(x1_ok[t], 1)
                for c in range(CH):
                    b, col = ((2, 4)[t] + c // 4, (c % 4) * P) if t < 2 else (0, c * n)
                    last = nc.tensor.transpose(bank[b][:, col:col + n], x[0:n, t, c * P:(c + 1) * P],
                                               ident[0:n, 0:n])
                last.then_inc(S["x1t_psum"], 1)

            def router(t):
                t0, n = TILES[t]
                pe.wait_ge(S["x1t_act"], t + 1)
                for c in range(CH):
                    j = c % 4
                    last = mm(bank[LOGIT_BANKS[t]][j * NE:(j + 1) * NE, 0:n], router_w[:, c, :], xT[:, c, t0:t0 + n],
                              start=c < 4, stop=c >= 4, tile_position=(0, j * NE), skip_group_check=True)
                last.then_inc(S["part_psum"], 1)

            def logit_sum(t):
                n = TILES[t][1]
                pe.wait_ge(S["part_ok"], t + 1)
                mm(bank[LOGIT_BANKS[t]][0:n, 0:NE], logit_part[:, t, 0:n], four_ident[:, :], start=True, stop=True)\
                    .then_inc(S["logit_psum"], 1)

            x1t(0)
            router(0)
            x1t(1)
            logit_sum(0)
            router(1)
            logit_sum(1)
            x1t(2)
            router(2)
            logit_sum(2)
            pe.wait_ge(S["states_sb"], 1)
            pe.wait_ge(S["chosen_ok"], 3)
            for t, (t0, n) in enumerate(TILES):
                for t2 in range(t):
                    mm(bank[6][:, t * NE:(t + 1) * NE], ones_bf[:, :], chosen[:, t2, :],
                       start=t2 == 0, stop=False)
                mm(bank[6][:, t * NE:(t + 1) * NE], earlier_bf[0:n, :], chosen[0:n, t, :],
                   start=t == 0, stop=True)
            for t, (t0, n) in enumerate(TILES):
                last = mm(bank[6][:, 3 * NE:4 * NE], ones_bf[0:n, :], chosen[0:n, t, :],
                          start=t == 0, stop=t == 2)
            last.then_inc(S["rank_psum"], 1)

            def gather():
                for t, (t0, n) in enumerate(TILES):
                    for side in range(2):
                        last = mm(bank[3][side * UT:(side + 1) * UT, :], member[0:n, t, :],
                                  x[0:n, t, side * HALF:(side + 1) * HALF], start=t == 0, stop=t == 2,
                                  skip_group_check=True)
                last.then_inc(S["gathered"], 1)

            def transposed(b, src, s):
                for c in range(4):
                    last = nc.tensor.transpose(bank[b][:, c * P:(c + 1) * P], src[:, c * P:(c + 1) * P], ident[:, :])
                last.then_inc(S[s], 1)

            pe.wait_ge(S["member_ok"], 1)
            gather()
            pe.wait_ge(S["expert_col_ok"], 1)
            mm(bank[7][0:1, 0:TABW], expert_col[0:TABW, :], ident[0:TABW, 0:TABW], start=True, stop=True)\
                .then_inc(S["expert_psum"], 1)
            pe.wait_ge(S["rows_ok"], 1)
            transposed(3, x_rows, "xu_psum")

            pe.wait_ge(S["tab_ok"], 1)
            n_last = pe.value_load(last_unit[0:1, 0:1], min_val=NE - 1, max_val=MAXU - 1)

            def product(b, m, left, s, e, between=None):
                for hf in range(2):
                    pe.wait_ge(slot_loaded[2 * m + hf], e * 16 + 16 * (PRIOR[2 * m + hf] + 1))
                    w = slot(2 * m + hf)
                    for c in range(4):
                        lhsT = left[:, c * P + hf * UT:c * P + hf * UT + UT]
                        end = hf == 1 and c == 3
                        for side in range(2):
                            last = mm(bank[b][side * UT:(side + 1) * UT, :], lhsT,
                                      w[:, c, side * HALF:(side + 1) * HALF], start=False, stop=end,
                                      skip_group_check=True)
                    if hf == 0:
                        last.then_inc(half_used[m], 1)
                        if between:
                            between()
                last.then_inc(S[s], 1)

            def biased(b, m):
                sel, rows = (part_sel, bias_parts[:, m, :]) if m < 2 else (half_sel, bias_rows[0:2, m, :])
                return mm(bank[b][:, :], sel[:, :], rows, start=True, stop=False, skip_group_check=True)

            def combine(u, order):
                pe.wait_ge(S["spread_ok"], u + 1)
                pe.wait_ge(S["y_ok"], u + 1)
                for t in order:
                    t0, n = TILES[t]
                    for h_ in range(2):
                        b = bank[SUM_BANKS[t][h_]]
                        last = mm(b[0:n, :] if t < 2 else b[UT * h_:UT * h_ + UT, :],
                                  spread[UT * h_:UT * h_ + UT, t0:t0 + n], y_rows[UT * h_:UT * h_ + UT, :],
                                  start=True, stop=True, skip_group_check=True)
                    last.then_inc(S["combined"], 1)

            def unit(u, e, before=None):
                pe.wait_ge(S["xu_ok"], u + 1)
                pe.wait_ge(S["gu_split"], u + 1)
                pe.wait_ge(S["gate_free"], u + 1)
                biased(0, 0)
                product(0, 0, xTu, "gate_done", e,
                        between=None if before is None else lambda: combine(before, SUM_ORDER))
                if before is not None:
                    pe.wait_ge(S["total_ok"], before * 3 + 2)
                biased(1, 1).then_inc(S["gu_bias_used"], 1)
                product(1, 1, xTu, "up_done", e)
                if before is not None:
                    pe.wait_ge(S["total_ok"], before * 3 + 3)
                pe.wait_ge(S["gated_ok"], u + 1)
                for t, (t0, n) in enumerate(TILES):
                    last = nc.tensor.transpose(bank[5][:, t0:t0 + n], gated[0:n, t, :], ident[0:n, 0:n])
                last.then_inc(S["spread_psum"], 1)
                pe.wait_ge(S["member_ok"], u + 2)
                gather()
                pe.wait_ge(S["down_bias_in"], u * 16 + 16)
                biased(2, 2).then_inc(S["down_bias_used"], 1)
                pe.wait_ge(S["hid_ok"], u + 1)
                transposed(4, hid, "hu_psum")
                pe.wait_ge(S["rows_ok"], u + 2)
                transposed(3, x_rows, "xu_psum")
                pe.wait_ge(S["hu_ok"], u + 1)
                product(2, 2, hTu, "y_done", e)

            pe.wait_ge(S["sel_ok"], 3)
            unit(0, 0)
            with pe.Fori(0, n_last) as before:
                e = pe.value_load(unit_expert[0:1, bass.ds(before + 1, 1)], min_val=0, max_val=NE - 1)
                unit(before + 1, e, before)
            combine(n_last, (0, 1, 2))


_INS = ["x_prompt", "x_sample", "state_conv_a", "state_conv_b", "state_lru_h", "w_in", "conv_a_w", "conv_b_w",
        "conv_b_b", "lru_wa", "lru_ba", "lru_wi", "lru_bi", "lru_lambda", "gn_a", "gn_b", "w_out", "ln1_g", "ln1_b",
        "router_w", "router_b", "exp_w_gate", "exp_b_gate", "exp_w_up", "exp_b_up", "exp_w_down", "exp_b_down",
        "ln2_g", "ln2_b"]
_OUTS = [("y_prompt", (1, SEQ, D)), ("y_sample", (NB, DS, D)), ("prompt_conv_a", (1, 1, 2, CW)),
         ("prompt_conv_b", (1, 1, 3, CW)), ("prompt_lru_h", (1, 1, CW)), ("sample_conv_a", (1, NB, 2, CW)),
         ("sample_conv_b", (1, NB, 3, CW)), ("sample_lru_h", (1, NB, CW))]


def kernel(**inputs):
    import numpy as np
    import concourse.bacc as bacc
    from concourse.bass_utils import run_bass_kernel_spmd

    nc = bacc.Bacc("TRN2", target_bir_lowering=False, num_devices=1)
    arrays, args = {}, {}
    for name in _INS:
        v = np.ascontiguousarray(inputs[name])
        arrays[f"in_{name}"] = v
        args[name] = nc.dram_tensor(f"in_{name}", v.shape, mybir.dt.from_np(v.dtype), kind="ExternalInput").ap()
    for name, shape in _OUTS:
        args[name] = nc.dram_tensor(f"out_{name}", shape, mybir.dt.float32, kind="ExternalOutput").ap()
    hybrid_layer(nc, args)
    r = run_bass_kernel_spmd(nc, [arrays], core_ids=[0])
    return tuple(r.results[0][f"out_{name}"] for name, _ in _OUTS)
```
